# Optimizing a Trainium2 kernel written in Bass

```python
import jax
import jax.numpy as jnp
from jax import lax
import numpy as np
import math
import jax, jax.numpy as jnp

D_MODEL = 1024
BATCH = 1
SEQ = 256
DEPTH = 1

N_MEM = 256
EPS = 1e-6

GLA_HEADS = 4
GLA_DK = D_MODEL // 16
GLA_DV = D_MODEL // 8
GLA_RANK = 16
GLA_GATE_NORMALIZER = 16.0
GLA_CHUNK = 64

MOBA_HEADS = 4
MOBA_DH = D_MODEL // 16
MOBA_BLOCK = 256
MOBA_TOPK = 3
MOBA_QBLOCK = 128

MEM_HEADS = 4
MEM_DH = D_MODEL // 16

GLA_QK_W = GLA_HEADS * GLA_DK
GLA_V_W = GLA_HEADS * GLA_DV
MOBA_W = MOBA_HEADS * MOBA_DH
MEM_W = MEM_HEADS * MEM_DH
D_MIX = GLA_V_W + MOBA_W + MEM_W
IN_SPLITS = (GLA_QK_W, GLA_QK_W, GLA_V_W, GLA_V_W, GLA_RANK, MOBA_W, MOBA_W, MOBA_W, MEM_W)
D_IN = sum(IN_SPLITS)

N_GROUPS = 4
EXPERTS_PER_GROUP = 8
N_EXPERTS = N_GROUPS * EXPERTS_PER_GROUP
MOE_TOPK = 2
MOE_FF = D_MODEL // 2
MOE_BLOCK = 128


def rmsnorm(x, g):
    xf = x.astype(jnp.float32)
    y = xf * lax.rsqrt(jnp.mean(xf * xf, axis=-1, keepdims=True) + EPS)
    return (y * g.astype(jnp.float32)).astype(x.dtype)

def split_heads(t, n):
    b, s, w = t.shape
    return t.reshape(b, s, n, w // n).transpose(0, 2, 1, 3)

def merge_heads(t):
    b, n, s, d = t.shape
    return t.transpose(0, 2, 1, 3).reshape(b, s, n * d)

def alibi_slopes(n):
    return jnp.asarray(2.0 ** (-8.0 * np.arange(1, n + 1) / n), dtype=jnp.float32)

def gla_chunked(q, k, v, g):
    f32 = jnp.float32
    b, h, s, dk = q.shape
    dv = v.shape[-1]
    c = GLA_CHUNK
    n = s // c
    qf = q.astype(f32).reshape(b, h, n, c, dk) * (dk ** -0.5)
    kf = k.astype(f32).reshape(b, h, n, c, dk)
    vf = v.astype(f32).reshape(b, h, n, c, dv)
    cum = jnp.cumsum(g.astype(f32).reshape(b, h, n, c, dk), axis=3)
    cum_last = cum[:, :, :, -1:, :]
    q_dec = qf * jnp.exp(cum)
    k_inv = kf * jnp.exp(-cum)
    causal = jnp.tril(jnp.ones((c, c), dtype=bool))
    a_intra = jnp.where(causal, jnp.einsum('bhnik,bhnjk->bhnij', q_dec, k_inv), 0.0)
    o_intra = jnp.einsum('bhnij,bhnjv->bhniv', a_intra, vf)
    k_end = kf * jnp.exp(cum_last - cum)
    d_state = jnp.einsum('bhnck,bhncv->nbhkv', k_end, vf)
    chunk_decay = jnp.moveaxis(jnp.exp(cum_last[:, :, :, 0, :]), 2, 0)

    def step(state, inp):
        dec, ds = inp
        return state * dec[..., None] + ds, state

    _, s_prev = lax.scan(step, jnp.zeros((b, h, dk, dv), f32), (chunk_decay, d_state))
    o_inter = jnp.einsum('bhnck,nbhkv->bhncv', q_dec, s_prev)
    return (o_intra + o_inter).reshape(b, h, s, dv)

def moba_attention(q, k, v, slopes):
    f32 = jnp.float32
    b, h, s, d = q.shape
    nb = -(-s // MOBA_BLOCK)
    pad = nb * MOBA_BLOCK - s
    k_p = jnp.pad(k, ((0, 0), (0, 0), (0, pad), (0, 0)))
    v_p = jnp.pad(v, ((0, 0), (0, 0), (0, pad), (0, 0)))
    kb = k_p.reshape(b, h, nb, MOBA_BLOCK, d)
    vb = v_p.reshape(b, h, nb, MOBA_BLOCK, d)
    k_mean = jnp.mean(kb.astype(f32), axis=3)
    nb_gate = max(nb, MOBA_TOPK)
    scale = d ** -0.5
    bi = jnp.arange(b)[:, None, None, None]
    hi = jnp.arange(h)[None, :, None, None]
    blk_pos = jnp.arange(MOBA_BLOCK)
    m = slopes[None, :, None, None]
    n_sel = MOBA_TOPK * MOBA_BLOCK

    def query_block(qb):
        start = qb * MOBA_QBLOCK
        qc = lax.dynamic_slice_in_dim(q, start, MOBA_QBLOCK, axis=2)
        t = start + jnp.arange(MOBA_QBLOCK)
        own = start // MOBA_BLOCK
        gate = jnp.einsum('bhqd,bhnd->bhqn', qc.astype(f32), k_mean)
        gate = jnp.where(jnp.arange(nb) < own, gate, -jnp.inf)
        gate = jnp.pad(gate, ((0, 0), (0, 0), (0, 0), (0, nb_gate - nb)), constant_values=-jnp.inf)
        _, idx = lax.top_k(gate, MOBA_TOPK)
        idx = jnp.minimum(idx, nb - 1)
        valid = jnp.arange(MOBA_TOPK) < own
        k_sel = kb[bi, hi, idx]
        v_sel = vb[bi, hi, idx]
        s_sel = jnp.einsum('bhqd,bhqkjd->bhqkj', qc, k_sel, preferred_element_type=f32) * scale
        dist_sel = (t[:, None, None] - (idx[..., None] * MOBA_BLOCK + blk_pos)).astype(f32)
        s_sel = jnp.where(valid[:, None], s_sel - m[..., None] * dist_sel, -jnp.inf)
        k_own = lax.dynamic_slice_in_dim(k_p, own * MOBA_BLOCK, MOBA_BLOCK, axis=2)
        v_own = lax.dynamic_slice_in_dim(v_p, own * MOBA_BLOCK, MOBA_BLOCK, axis=2)
        dist_own = (t[:, None] - (own * MOBA_BLOCK + blk_pos)[None, :]).astype(f32)
        s_own = jnp.einsum('bhqd,bhjd->bhqj', qc, k_own, preferred_element_type=f32) * scale
        s_own = jnp.where(dist_own >= 0, s_own - m * dist_own, -jnp.inf)
        scores = jnp.concatenate([s_sel.reshape(b, h, MOBA_QBLOCK, n_sel), s_own], axis=-1)
        p = jax.nn.softmax(scores, axis=-1)
        p_sel = p[..., :n_sel].reshape(b, h, MOBA_QBLOCK, MOBA_TOPK, MOBA_BLOCK).astype(v.dtype)
        p_own = p[..., n_sel:].astype(v.dtype)
        o = (jnp.einsum('bhqkj,bhqkjd->bhqd', p_sel, v_sel, preferred_element_type=f32)
             + jnp.einsum('bhqj,bhjd->bhqd', p_own, v_own, preferred_element_type=f32))
        return o.astype(q.dtype)

    out = lax.map(query_block, jnp.arange(s // MOBA_QBLOCK))
    return out.transpose(1, 2, 0, 3, 4).reshape(b, h, s, d)

def memory_attention(q, mk, mv):
    f32 = jnp.float32
    scale = q.shape[-1] ** -0.5
    s = jnp.einsum('bhsd,bhmd->bhsm', q, mk, preferred_element_type=f32) * scale
    p = jax.nn.softmax(s, axis=-1).astype(mv.dtype)
    return jnp.einsum('bhsm,bhmd->bhsd', p, mv, preferred_element_type=f32).astype(q.dtype)

def hierarchical_moe(h, w_rg, b_rg, w_re, b_re, w_gate, w_up, w_down):
    f32 = jnp.float32
    b, s, d = h.shape
    t_tok = b * s
    xt = h.reshape(t_tok, d)
    lg = jnp.einsum('td,dg->tg', xt, w_rg).astype(f32) + b_rg.astype(f32)
    g_sel = jnp.argmax(lg, axis=-1)
    p_group = jnp.take_along_axis(jax.nn.softmax(lg, axis=-1), g_sel[:, None], axis=-1)
    le = jnp.einsum('td,gde->tge', xt, w_re).astype(f32) + b_re.astype(f32)
    le = jnp.take_along_axis(le, g_sel[:, None, None], axis=1)[:, 0]
    le_top, e_loc = lax.top_k(le, MOE_TOPK)
    gates = p_group * jax.nn.softmax(le_top, axis=-1)
    expert = (g_sel[:, None] * EXPERTS_PER_GROUP + e_loc).astype(jnp.int32)

    n_assign = t_tok * MOE_TOPK
    e_flat = expert.reshape(n_assign)
    t_flat = jnp.repeat(jnp.arange(t_tok, dtype=jnp.int32), MOE_TOPK)
    w_flat = gates.reshape(n_assign)
    order = jnp.argsort(e_flat)
    e_s, t_s, w_s = e_flat[order], t_flat[order], w_flat[order]
    counts = jax.ops.segment_sum(jnp.ones((n_assign,), jnp.int32), e_flat, num_segments=N_EXPERTS)
    padded = (counts + MOE_BLOCK - 1) // MOE_BLOCK * MOE_BLOCK
    starts = jnp.cumsum(counts) - counts
    pstarts = jnp.cumsum(padded) - padded
    dest = pstarts[e_s] + (jnp.arange(n_assign, dtype=jnp.int32) - starts[e_s])
    n_blocks = (n_assign + N_EXPERTS * (MOE_BLOCK - 1) + MOE_BLOCK - 1) // MOE_BLOCK
    n_rows = n_blocks * MOE_BLOCK
    tok_buf = jnp.full((n_rows,), t_tok, jnp.int32).at[dest].set(t_s)
    w_buf = jnp.zeros((n_rows,), f32).at[dest].set(w_s)
    block_start = jnp.arange(n_blocks, dtype=jnp.int32) * MOE_BLOCK
    block_expert = jnp.minimum(jnp.searchsorted(pstarts + padded, block_start, side='right'), N_EXPERTS - 1)
    x_pad = jnp.concatenate([xt, jnp.zeros((1, d), xt.dtype)], axis=0)

    def expert_block(args):
        toks, e = args
        xb = x_pad[toks]
        hid = jax.nn.silu(xb @ w_gate[e]) * (xb @ w_up[e])
        return hid @ w_down[e]

    y = lax.map(expert_block, (tok_buf.reshape(n_blocks, MOE_BLOCK), block_expert))
    y = y.reshape(n_rows, d) * w_buf[:, None].astype(y.dtype)
    out = jnp.zeros((t_tok + 1, d), y.dtype).at[tok_buf].add(y)[:t_tok]
    return out.reshape(b, s, d)

def first_inputs(seed: int = 0) -> dict:
    key = jax.random.key(seed)
    ks = jax.random.split(key, 24)
    L = DEPTH

    def nrm(k, shape, fan_in):
        return jax.random.normal(k, shape, jnp.float32) * fan_in ** -0.5

    def gain(k, shape):
        return 1.0 + 0.02 * jax.random.normal(k, shape, jnp.float32)

    return {
        'x': jax.random.normal(ks[0], (BATCH, SEQ, D_MODEL), jnp.float32),
        'mem': jax.random.normal(ks[1], (BATCH, N_MEM, D_MODEL), jnp.float32),
        'attn_norm_g': gain(ks[2], (L, D_MODEL)),
        'mem_norm_g': gain(ks[3], (L, D_MODEL)),
        'w_in': nrm(ks[4], (L, D_MODEL, D_IN), D_MODEL),
        'w_gla_gk': nrm(ks[5], (L, GLA_RANK, GLA_QK_W), GLA_RANK),
        'b_gla_gk': 0.1 * jax.random.normal(ks[6], (L, GLA_QK_W), jnp.float32),
        'gla_out_norm_g': gain(ks[7], (L, GLA_DV)),
        'moba_q_norm_g': gain(ks[8], (L, MOBA_DH)),
        'moba_k_norm_g': gain(ks[9], (L, MOBA_DH)),
        'w_mem_kv': nrm(ks[10], (L, D_MODEL, 2 * MEM_W), D_MODEL),
        'mem_q_norm_g': gain(ks[11], (L, MEM_DH)),
        'mem_k_norm_g': gain(ks[12], (L, MEM_DH)),
        'w_out': nrm(ks[13], (L, D_MIX, D_MODEL), D_MIX),
        'ffn_norm_g': gain(ks[14], (L, D_MODEL)),
        'w_router_group': nrm(ks[15], (L, D_MODEL, N_GROUPS), D_MODEL),
        'b_router_group': 0.01 * jax.random.normal(ks[16], (L, N_GROUPS), jnp.float32),
        'w_router_expert': nrm(ks[17], (L, N_GROUPS, D_MODEL, EXPERTS_PER_GROUP), D_MODEL),
        'b_router_expert': 0.01 * jax.random.normal(ks[18], (L, N_GROUPS, EXPERTS_PER_GROUP), jnp.float32),
        'w_gate': nrm(ks[19], (L, N_EXPERTS, D_MODEL, MOE_FF), D_MODEL),
        'w_up': nrm(ks[20], (L, N_EXPERTS, D_MODEL, MOE_FF), D_MODEL),
        'w_down': nrm(ks[21], (L, N_EXPERTS, MOE_FF, D_MODEL), MOE_FF),
    }

def first_block(x, mem, attn_norm_g, mem_norm_g, w_in, w_gla_gk, b_gla_gk, gla_out_norm_g,
              moba_q_norm_g, moba_k_norm_g, w_mem_kv, mem_q_norm_g, mem_k_norm_g, w_out,
              ffn_norm_g, w_router_group, b_router_group, w_router_expert, b_router_expert,
              w_gate, w_up, w_down):
    slopes = alibi_slopes(MOBA_HEADS)
    split_at = np.cumsum(IN_SPLITS)[:-1].tolist()
    for l in range(DEPTH):
        h = rmsnorm(x, attn_norm_g[l])
        proj = jnp.einsum('bsd,de->bse', h, w_in[l])
        gla_q, gla_k, gla_v, gla_r, gla_lr, mb_q, mb_k, mb_v, mem_q = jnp.split(proj, split_at, axis=-1)

        g_log = jax.nn.log_sigmoid((gla_lr @ w_gla_gk[l] + b_gla_gk[l]).astype(jnp.float32)) / GLA_GATE_NORMALIZER
        o_gla = gla_chunked(split_heads(gla_q, GLA_HEADS), split_heads(gla_k, GLA_HEADS),
                            split_heads(gla_v, GLA_HEADS), split_heads(g_log, GLA_HEADS))
        o_gla = rmsnorm(o_gla, gla_out_norm_g[l]).astype(x.dtype)
        o_gla = merge_heads(o_gla) * jax.nn.silu(gla_r)

        q_b = rmsnorm(split_heads(mb_q, MOBA_HEADS), moba_q_norm_g[l])
        k_b = rmsnorm(split_heads(mb_k, MOBA_HEADS), moba_k_norm_g[l])
        v_b = split_heads(mb_v, MOBA_HEADS)
        o_moba = merge_heads(moba_attention(q_b, k_b, v_b, slopes))

        mem_h = rmsnorm(mem, mem_norm_g[l])
        mem_k, mem_v = jnp.split(jnp.einsum('bmd,de->bme', mem_h, w_mem_kv[l]), 2, axis=-1)
        q_c = rmsnorm(split_heads(mem_q, MEM_HEADS), mem_q_norm_g[l])
        k_c = rmsnorm(split_heads(mem_k, MEM_HEADS), mem_k_norm_g[l])
        o_mem = merge_heads(memory_attention(q_c, k_c, split_heads(mem_v, MEM_HEADS)))

        mix = jnp.concatenate([o_gla, o_moba, o_mem], axis=-1)
        x = x + jnp.einsum('bse,ed->bsd', mix, w_out[l])

        x = x + hierarchical_moe(rmsnorm(x, ffn_norm_g[l]), w_router_group[l], b_router_group[l],
                                 w_router_expert[l], b_router_expert[l], w_gate[l], w_up[l], w_down[l])
    return x


DEPTH_2 = 2

N_MIXERS = 2
N_ATTN_LAYERS = (DEPTH_2 + 1) // 2
N_SSM_LAYERS = DEPTH_2 // 2

HEAD_DIM = 64
N_HEADS = D_MODEL // (2 * HEAD_DIM)
Q_BLOCK = 128

REL_BUCKETS = 32
REL_MAX_DIST = 128

GROUP_CH = 16
GROUPS = D_MODEL // GROUP_CH
SSM_STATE = 64
SSM_CHUNK = 128

D_FF = 2816
FFN_RESIDUAL = 0.5

PLE_DIM = 256

N_NORMS = 8
RMS_EPS = 1e-6
NEG_INF = -1e30


def rmsnorm_2(x, g):
    xf = x.astype(jnp.float32)
    y = xf * lax.rsqrt(jnp.mean(xf * xf, axis=-1, keepdims=True) + RMS_EPS)
    return (y * g.astype(jnp.float32)).astype(x.dtype)

def swiglu(h, w_in, w_out):
    gu = h @ w_in
    return (jax.nn.silu(gu[..., :D_FF]) * gu[..., D_FF:]) @ w_out

def t5_bucket(n):
    n = jnp.maximum(n, 0)
    max_exact = REL_BUCKETS // 2
    nf = jnp.maximum(n, 1).astype(jnp.float32)
    large = max_exact + (jnp.log(nf / max_exact) / math.log(REL_MAX_DIST / max_exact)
                         * (REL_BUCKETS - max_exact)).astype(jnp.int32)
    large = jnp.minimum(large, REL_BUCKETS - 1)
    return jnp.where(n < max_exact, n, large)

def diff_attention(h, w_qkv, w_o, lam_vecs, subln_g, rel_bias, lambda_init):
    Bsz, S, _ = h.shape
    n_blk = S // Q_BLOCK
    qkv = h @ w_qkv
    q, k, v = jnp.split(qkv, 3, axis=-1)
    q = q.reshape(Bsz, S, N_HEADS, 2, HEAD_DIM).transpose(0, 2, 3, 1, 4) * (HEAD_DIM ** -0.5)
    k = k.reshape(Bsz, S, N_HEADS, 2, HEAD_DIM).transpose(0, 2, 3, 1, 4)
    v = v.reshape(Bsz, S, N_HEADS, 2 * HEAD_DIM).transpose(0, 2, 1, 3)

    lv = lam_vecs.astype(jnp.float32)
    lam = jnp.exp(jnp.sum(lv[0] * lv[1])) - jnp.exp(jnp.sum(lv[2] * lv[3])) + lambda_init

    q_blocks = jnp.moveaxis(q.reshape(Bsz, N_HEADS, 2, n_blk, Q_BLOCK, HEAD_DIM), 3, 0)
    k_pos = jnp.arange(S, dtype=jnp.int32)

    def block(args):
        q_blk, blk = args
        q_pos = blk * Q_BLOCK + jnp.arange(Q_BLOCK, dtype=jnp.int32)
        dist = q_pos[:, None] - k_pos[None, :]
        bias = rel_bias.astype(jnp.float32)[t5_bucket(dist)]
        bias = bias.reshape(Q_BLOCK, S, N_HEADS, 2).transpose(2, 3, 0, 1)
        s = jnp.einsum('bhmqd,bhmkd->bhmqk', q_blk, k).astype(jnp.float32) + bias
        s = jnp.where(dist >= 0, s, NEG_INF)
        prob = jax.nn.softmax(s, axis=-1)
        attn = prob[:, :, 0] - lam * prob[:, :, 1]
        return jnp.einsum('bhqk,bhkv->bhqv', attn.astype(v.dtype), v)

    o = lax.map(block, (q_blocks, jnp.arange(n_blk, dtype=jnp.int32)))
    o = jnp.moveaxis(o, 0, 2).reshape(Bsz, N_HEADS, S, 2 * HEAD_DIM)
    o = rmsnorm_2(o, subln_g) * (1.0 - lambda_init)
    o = o.transpose(0, 2, 1, 3).reshape(Bsz, S, D_MODEL)
    return o @ w_o

def s5_glu(h, lam_re, lam_im, log_dt, b_re, b_im, c_re, c_im, d_skip, w_glu, b_glu):
    Bsz, S, _ = h.shape
    n_chunks = S // SSM_CHUNK
    lam = lax.complex(lam_re.astype(jnp.float32), lam_im.astype(jnp.float32))
    dt = jnp.exp(log_dt.astype(jnp.float32))[:, None]
    lam_dt = lam * dt
    a_bar = jnp.exp(lam_dt)
    b = lax.complex(b_re.astype(jnp.float32), b_im.astype(jnp.float32))
    b_bar = ((a_bar - 1.0) / lam)[:, :, None] * b
    c = lax.complex(c_re.astype(jnp.float32), c_im.astype(jnp.float32))
    d_g = d_skip.astype(jnp.float32).reshape(GROUPS, GROUP_CH)
    steps = jnp.arange(1, SSM_CHUNK + 1, dtype=jnp.float32)
    a_pow = jnp.exp(steps[:, None, None] * lam_dt[None])

    u = h.astype(jnp.float32).reshape(Bsz, n_chunks, SSM_CHUNK, GROUPS, GROUP_CH)
    u = jnp.moveaxis(u, 1, 0)

    def combine(e1, e2):
        a1, x1 = e1
        a2, x2 = e2
        return a1 * a2, a2 * x1 + x2

    def chunk_step(state, u_c):
        bu = jnp.einsum('gph,bcgh->bcgp', b_bar, u_c.astype(jnp.complex64))
        a = jnp.broadcast_to(a_bar, bu.shape)
        _, xs = lax.associative_scan(combine, (a, bu), axis=1)
        xs = xs + a_pow[None] * state[:, None]
        y = jnp.einsum('ghp,bcgp->bcgh', c, xs).real + d_g * u_c
        return xs[:, -1], y

    state0 = jnp.zeros((Bsz, GROUPS, SSM_STATE), jnp.complex64)
    _, ys = lax.scan(chunk_step, state0, u)
    y = jnp.moveaxis(ys, 0, 1).reshape(Bsz, S, D_MODEL).astype(h.dtype)
    z = jax.nn.gelu(y) @ w_glu + b_glu
    return z[..., :D_MODEL] * jax.nn.sigmoid(z[..., D_MODEL:])

def second_inputs(seed: int = 0) -> dict:
    key = jax.random.key(seed)
    ks = jax.random.split(key, 24)
    f32 = jnp.float32
    nrm = lambda k, shape, scale: jax.random.normal(k, shape, f32) * scale

    x = nrm(ks[0], (BATCH, SEQ, D_MODEL), 1.0)
    p = nrm(ks[1], (DEPTH_2, BATCH, SEQ, PLE_DIM), 1.0)
    norm_g = 1.0 + nrm(ks[2], (DEPTH_2, N_NORMS, D_MODEL), 0.05)
    ffn_w_in = nrm(ks[3], (DEPTH_2, 2, D_MODEL, 2 * D_FF), D_MODEL ** -0.5)
    ffn_w_out = nrm(ks[4], (DEPTH_2, 2, D_FF, D_MODEL), D_FF ** -0.5)

    attn_w_qkv = nrm(ks[5], (N_ATTN_LAYERS, D_MODEL, 3 * D_MODEL), D_MODEL ** -0.5)
    attn_w_o = nrm(ks[6], (N_ATTN_LAYERS, D_MODEL, D_MODEL), D_MODEL ** -0.5)
    attn_lam = nrm(ks[7], (N_ATTN_LAYERS, 4, HEAD_DIM), 0.1)
    attn_subln_g = 1.0 + nrm(ks[8], (N_ATTN_LAYERS, 2 * HEAD_DIM), 0.05)
    rel_bias = nrm(ks[9], (REL_BUCKETS, 2 * N_HEADS), 0.5)

    n_idx = jnp.arange(SSM_STATE, dtype=f32)
    ssm_lam_re = jnp.full((N_SSM_LAYERS, GROUPS, SSM_STATE), -0.5, f32) + nrm(ks[10], (N_SSM_LAYERS, GROUPS, SSM_STATE), 1e-3)
    ssm_lam_im = jnp.broadcast_to(math.pi * n_idx, (N_SSM_LAYERS, GROUPS, SSM_STATE)) + nrm(ks[11], (N_SSM_LAYERS, GROUPS, SSM_STATE), 1e-3)
    ssm_log_dt = jax.random.uniform(ks[12], (N_SSM_LAYERS, GROUPS), f32, math.log(1e-3), math.log(1e-1))
    b_scale = (2.0 * GROUP_CH) ** -0.5
    c_scale = (2.0 * SSM_STATE) ** -0.5
    ssm_b_re = nrm(ks[13], (N_SSM_LAYERS, GROUPS, SSM_STATE, GROUP_CH), b_scale)
    ssm_b_im = nrm(ks[14], (N_SSM_LAYERS, GROUPS, SSM_STATE, GROUP_CH), b_scale)
    ssm_c_re = nrm(ks[15], (N_SSM_LAYERS, GROUPS, GROUP_CH, SSM_STATE), c_scale)
    ssm_c_im = nrm(ks[16], (N_SSM_LAYERS, GROUPS, GROUP_CH, SSM_STATE), c_scale)
    ssm_d = nrm(ks[17], (N_SSM_LAYERS, D_MODEL), 1.0)
    ssm_w_glu = nrm(ks[18], (N_SSM_LAYERS, D_MODEL, 2 * D_MODEL), D_MODEL ** -0.5)
    ssm_b_glu = nrm(ks[19], (N_SSM_LAYERS, 2 * D_MODEL), 0.01)

    ple_w_proj = nrm(ks[20], (DEPTH_2, PLE_DIM, D_MODEL), PLE_DIM ** -0.5)
    ple_w_gate = nrm(ks[21], (DEPTH_2, D_MODEL, D_MODEL), D_MODEL ** -0.5)

    return {"x": x, "p": p, "norm_g": norm_g, "ffn_w_in": ffn_w_in, "ffn_w_out": ffn_w_out,
            "attn_w_qkv": attn_w_qkv, "attn_w_o": attn_w_o, "attn_lam": attn_lam,
            "attn_subln_g": attn_subln_g, "rel_bias": rel_bias,
            "ssm_lam_re": ssm_lam_re, "ssm_lam_im": ssm_lam_im, "ssm_log_dt": ssm_log_dt,
            "ssm_b_re": ssm_b_re, "ssm_b_im": ssm_b_im, "ssm_c_re": ssm_c_re, "ssm_c_im": ssm_c_im,
            "ssm_d": ssm_d, "ssm_w_glu": ssm_w_glu, "ssm_b_glu": ssm_b_glu,
            "ple_w_proj": ple_w_proj, "ple_w_gate": ple_w_gate}

def second_block(x, p, norm_g, ffn_w_in, ffn_w_out, attn_w_qkv, attn_w_o, attn_lam, attn_subln_g,
              rel_bias, ssm_lam_re, ssm_lam_im, ssm_log_dt, ssm_b_re, ssm_b_im, ssm_c_re, ssm_c_im,
              ssm_d, ssm_w_glu, ssm_b_glu, ple_w_proj, ple_w_gate):
    for i in range(DEPTH_2):
        g = norm_g[i]
        x = x + FFN_RESIDUAL * rmsnorm_2(swiglu(rmsnorm_2(x, g[0]), ffn_w_in[i, 0], ffn_w_out[i, 0]), g[1])
        h = rmsnorm_2(x, g[2])
        j = i // N_MIXERS
        if i % N_MIXERS == 0:
            lambda_init = 0.8 - 0.6 * math.exp(-0.3 * i)
            m = diff_attention(h, attn_w_qkv[j], attn_w_o[j], attn_lam[j], attn_subln_g[j],
                               rel_bias, lambda_init)
        else:
            m = s5_glu(h, ssm_lam_re[j], ssm_lam_im[j], ssm_log_dt[j], ssm_b_re[j], ssm_b_im[j],
                       ssm_c_re[j], ssm_c_im[j], ssm_d[j], ssm_w_glu[j], ssm_b_glu[j])
        x = x + rmsnorm_2(m, g[3])
        x = x + FFN_RESIDUAL * rmsnorm_2(swiglu(rmsnorm_2(x, g[4]), ffn_w_in[i, 1], ffn_w_out[i, 1]), g[5])
        gate = jax.nn.sigmoid(rmsnorm_2(x, g[6]) @ ple_w_gate[i])
        x = x + rmsnorm_2(gate * (p[i] @ ple_w_proj[i]), g[7])
    return x


def setup_inputs(seed=0):
    out = dict(first_inputs(seed))
    for name, value in second_inputs(seed + 1).items():
        if name != "x":
            out[name + "_2"] = value
    return out


def reference(
    x, mem, attn_norm_g, mem_norm_g, w_in, w_gla_gk, b_gla_gk, gla_out_norm_g, moba_q_norm_g,
    moba_k_norm_g, w_mem_kv, mem_q_norm_g, mem_k_norm_g, w_out, ffn_norm_g, w_router_group,
    b_router_group, w_router_expert, b_router_expert, w_gate, w_up, w_down, p_2, norm_g_2,
    ffn_w_in_2, ffn_w_out_2, attn_w_qkv_2, attn_w_o_2, attn_lam_2, attn_subln_g_2, rel_bias_2,
    ssm_lam_re_2, ssm_lam_im_2, ssm_log_dt_2, ssm_b_re_2, ssm_b_im_2, ssm_c_re_2, ssm_c_im_2,
    ssm_d_2, ssm_w_glu_2, ssm_b_glu_2, ple_w_proj_2, ple_w_gate_2,
):
    x = first_block(
        x, mem, attn_norm_g, mem_norm_g, w_in, w_gla_gk, b_gla_gk, gla_out_norm_g,
        moba_q_norm_g, moba_k_norm_g, w_mem_kv, mem_q_norm_g, mem_k_norm_g, w_out, ffn_norm_g,
        w_router_group, b_router_group, w_router_expert, b_router_expert, w_gate, w_up, w_down,
    )
    return second_block(
        x, p_2, norm_g_2, ffn_w_in_2, ffn_w_out_2, attn_w_qkv_2, attn_w_o_2, attn_lam_2,
        attn_subln_g_2, rel_bias_2, ssm_lam_re_2, ssm_lam_im_2, ssm_log_dt_2, ssm_b_re_2,
        ssm_b_im_2, ssm_c_re_2, ssm_c_im_2, ssm_d_2, ssm_w_glu_2, ssm_b_glu_2, ple_w_proj_2,
        ple_w_gate_2,
    )


_drawn_inputs = setup_inputs


def setup_inputs(seed=0):
    import zlib

    import numpy as np

    out = dict(_drawn_inputs(seed))
    spreads = {}
    factors = {'mem_norm_g': 8.0,
     'gla_out_norm_g': 22.44,
     'moba_q_norm_g': 31.181,
     'moba_k_norm_g': 27.407,
     'mem_q_norm_g': 8.0,
     'mem_k_norm_g': 8.0,
     'b_router_group': 51.615,
     'b_router_expert': 24.718,
     'ssm_lam_re_2': 200.0,
     'ssm_c_re_2': 123.528,
     'ssm_c_im_2': 124.536,
     'ssm_b_glu_2': 64.0,
     'b_gla_gk': 3.259,
     'ffn_norm_g': 7.601,
     'attn_subln_g_2': 43.768,
     'ssm_lam_im_2': 33.328,
     'ssm_log_dt_2': 37.248,
     'ssm_b_re_2': 45.736,
     'ssm_b_im_2': 45.584,
     'norm_g_2': 8.0,
     'attn_lam_2': 8.0,
     'rel_bias_2': 5.897,
     'ple_w_gate_2': 3.753}
    for name, (base, spread) in spreads.items():
        noise = np.random.default_rng([zlib.crc32(name.encode()), seed]).standard_normal(out[name].shape)
        drawn = base * np.exp(spread * noise) if base else spread * noise
        out[name] = jnp.asarray(drawn.astype(out[name].dtype))
    for name, factor in factors.items():
        out[name] = (out[name] * factor).astype(out[name].dtype)
    return out
```

```python
from contextlib import ExitStack
import math

import numpy as np
import concourse.bass as bass
from concourse import mybir

F32 = mybir.dt.float32
U32 = mybir.dt.uint32
ALU = mybir.AluOpType
ACT = mybir.ActivationFunctionType
AX = mybir.AxisListType

T = 256
D = 1024
NSLOT = 4
UNIT = 6144
NEXP = 32
FF_TILES = 22
NEG = -1e30
MAGIC = 12582912.0
TWO_PI = 2.0 * math.pi

SMALL = [
    ("attn_g", 8), ("mem_g", 8), ("ffn_g", 8), ("b_gk", 2), ("gla_g", 1), ("mbq_g", 1), ("mbk_g", 1),
    ("mq_g", 1), ("mk_g", 1), ("norm_g", 128), ("subln_g", 1), ("lam_re", 32), ("lam_im", 32),
    ("log_dt", 32), ("ssm_d", 8), ("b_glu", 16), ("lamv", 256), ("rbias", 36), ("w_r", 288),
    ("w_gk", 256), ("relb", 16),
]
CONST = [
    ("ident", 128), ("anti", 128), ("onesD", 128), ("onesB", 128), ("ones128", 128), ("mask", 128), ("tiew", 8),
    ("eps", 1), ("zero", 1), ("halfpi", 1), ("scanm", 256), ("tvec", 256), ("bucket", 512), ("cut", 512),
]


def columns(table):
    at, out = 0, {}
    for name, n in table:
        out[name] = (at, at + n)
        at += n
    return out, at


SCOL, NSC = columns(SMALL)
CCOL, NCC = columns(CONST)


class Eng:

    def __init__(self, name, sem):
        self.name, self.sem, self.n, self.q, self.seen = name, sem, 0, [], {}

    def wait(self, *toks):
        for t in toks:
            if t is None:
                continue
            sem, v = t
            if self.seen.get(id(sem), 0) >= v:
                continue
            self.seen[id(sem)] = v
            self.q.append(lambda e, sem=sem, v=v: e.wait_ge(sem, v))

    def do(self, fn, *toks, inc=True):
        self.wait(*toks)
        if inc:
            self.n += 1
            self.q.append(lambda e: fn(e).then_inc(self.sem, 1))
            return (self.sem, self.n)
        self.q.append(fn)
        return None

    @property
    def last(self):
        return (self.sem, self.n) if self.n else None


def program(nc, A, out, stage):
    with ExitStack() as ctx:
        def sb(name, shape, dt=F32):
            return ctx.enter_context(nc.sbuf_tensor(name, shape, dt))

        def sem(name):
            return ctx.enter_context(nc.semaphore(name))

        pe, act, dve, pool = (Eng(n, sem("s_" + n)) for n in ("pe", "act", "dve", "pool"))
        ring = sb("ring", [128, NSLOT, UNIT])
        s_ring = [sem(f"s_ring{i}") for i in range(NSLOT)]
        xT = sb("xT", [128, 8, T])
        hT = sb("hT", [128, 8, T])
        sq = sb("sq", [128, 8, T])
        small = sb("small", [128, NSC])
        cst = sb("cst", [128, NCC])
        rstd = sb("rstd", [128, 2, 2 * T])
        scr = sb("scr", [128, 18000])
        acc = ctx.enter_context(nc.psum_tensor("acc", [128, 4, 512], F32))
        wkt = [ctx.enter_context(nc.psum_tensor(f"wk{i}", [128, 512], F32)) for i in range(4)]

        def sm(name, a=0, b=None):
            s, e = SCOL[name]
            return small[:, s + a:(e if b is None else s + b)]

        def cs(name, a=0, b=None):
            s, e = CCOL[name]
            return cst[:, s + a:(e if b is None else s + b)]

        units = []
        released = {}

        def unit(src, ncols):
            n = len(units)
            units.append((src, ncols))
            s = n % NSLOT
            return n, ring[:, s, 0:ncols], (s_ring[s], 16 * (n // NSLOT + 1))

        def release(n, tok):
            released[n] = tok

        loads = []

        def load(dst, src, *toks):
            s = sem(f"s_ld{len(loads)}")
            loads.append(s)
            act.wait(*toks)
            act.q.append(lambda e: e.dma_start(dst, src).then_inc(s, 16))
            return (s, 16)

        wk_free = [None] * 4
        wk_at = [0]

        def bank():
            i = wk_at[0] % 4
            wk_at[0] += 1
            free = wk_free[i]
            assert free != "busy"
            wk_free[i] = "busy"
            return i, wkt[i], free

        acc_free = [None]

        def mm(out_, lhsT, rhs, start, stop, *toks, inc=False, skip=False):
            return pe.do(lambda e: e.matmul(out_, lhsT, rhs, start=start, stop=stop, skip_group_check=skip),
                         *toks, inc=inc)

        def tr(out_, in_, *toks, inc=False):
            return pe.do(lambda e: e.transpose(out_, in_, cs("ident")), *toks, inc=inc)

        def A_(out_, in_, func, *toks, **kw):
            return act.do(lambda e: e.activation(out_, in_, func, **kw), *toks, act.last)

        def tt(out_, a, b, op, *toks, eng=None):
            g = eng or dve
            return g.do(lambda e: e.tensor_tensor(out_, a, b, op), *toks, g.last)

        def ts(out_, a, s1, s2, op0, op1, *toks, eng=None):
            g = eng or dve
            if s2 is None:
                return g.do(lambda e: e.tensor_scalar(out_, a, s1, None, op0), *toks, g.last)
            return g.do(lambda e: e.tensor_scalar(out_, a, s1, s2, op0, op1), *toks, g.last)

        def stt(out_, a, s, b, op0, op1, *toks):
            return dve.do(lambda e: e.scalar_tensor_tensor(out=out_, in0=a, scalar=s, in1=b, op0=op0, op1=op1),
                          *toks, dve.last)

        def cp(out_, a, *toks):
            return dve.do(lambda e: e.tensor_copy(out_, a), *toks, dve.last)

        def memset(out_, v, *toks, eng=None):
            g = eng or dve
            return g.do(lambda e: e.memset(out_, v), *toks, g.last)

        def recip(out_, a, *toks):
            return dve.do(lambda e: e.reciprocal(out_, a), *toks, dve.last)

        def red(out_, a, op, *toks, negate=False, axis=AX.X):
            return dve.do(lambda e: e.tensor_reduce(out_, a, axis, op, negate=negate), *toks, dve.last)

        def fence():
            last = [g.last for g in (pe, act, dve, pool)]
            for g in (pe, act, dve, pool):
                g.wait(*last)

        MUL, ADD, SUB, MAX, MIN = ALU.mult, ALU.add, ALU.subtract, ALU.max, ALU.min

        t_x = load(xT[:, :, :], A["xT"].rearrange("(k p) t -> p k t", p=128))
        t_cst = load(cst[:, :], A["cst"])
        t_sm = load(small[:, :], A["small"])
        for g in (pe, act, dve, pool):
            g.wait(t_cst, t_sm)
        dve.wait(t_x)

        def bc(ap, n):
            return ap.rearrange("p (o t) -> p o t", o=1).broadcast_to([128, n, ap.shape[-1]])

        rs_free = [None, None]
        rs_at = [0]

        def stat(src, ones, ntile, groups, *toks):
            r = rs_at[0] % 2
            rs_at[0] += 1
            t = A_(sq[:, 0:ntile, :], src, ACT.Square, *toks, pe.last)
            i, b, free = bank()
            n = len(groups)
            for gi, grp in enumerate(groups):
                for k in grp:
                    tok = mm(b[:, gi * T:(gi + 1) * T], ones, sq[:, k, :], k == grp[0], k == grp[-1],
                             t, free, inc=True if k == grp[-1] else False)
            t = A_(rstd[:, r, 0:n * T], b[:, 0:n * T], ACT.Sqrt, tok, rs_free[r], bias=cs("eps"))
            wk_free[i] = t
            t = recip(rstd[:, r, 0:n * T], rstd[:, r, 0:n * T], t)
            return [rstd[:, r, g * T:(g + 1) * T] for g in range(n)], t, r

        def norm_in(dst, src, g, *toks):
            rs, t, r = stat(src[:, :, :], cs("onesD"), 8, [list(range(8))], dve.last, *toks)
            for k in range(8):
                t2 = stt(dst[:, k, :], src[:, k, :], g[:, k:k + 1], rs[0], MUL, MUL, t, pe.last)
            rs_free[r] = t2
            return t2

        def norm_add(src, g, *toks, half=False):
            rs, t, r = stat(src, cs("onesD"), 8, [list(range(8))], *toks)
            if half:
                ts(g, g, 0.5, None, MUL, None)
            for k in range(8):
                t2 = stt(hT[:, k, :], src[:, k, :], g[:, k:k + 1], rs[0], MUL, MUL, t, pe.last)
            acc_free[0] = t2
            rs_free[r] = t2
            return tt(xT[:, :, :], xT[:, :, :], hT[:, :, :], ADD, t2)

        def acc_tile(k):
            return acc[:, k // 2, (k % 2) * T:(k % 2 + 1) * T]

        acc3 = acc[:, :, :].rearrange("p b (h t) -> p (b h) t", t=T)

        def lin_fm(lhs, nk, rhs, ntiles, evac, *toks):
            for i0 in range(0, ntiles, 2):
                n = min(2, ntiles - i0)
                i, b, free = bank()
                for j in range(n):
                    for k in range(nk):
                        tok = mm(b[:, j * T:(j + 1) * T], lhs(k, i0 + j), rhs(k), k == 0, k == nk - 1,
                                 *toks, free, inc=(k == nk - 1 and j == n - 1))
                wk_free[i] = evac(i0, n, b, tok)

        def lin_acc(nk, lhs, rhs, *toks, k0=True, k1=True, tiles=range(8)):
            for k in range(nk):
                for d in tiles:
                    tok = mm(acc_tile(d), lhs(k, d), rhs(k), k0 and k == 0 and d % 2 == 0,
                             k1 and k == nk - 1, *toks, acc_free[0], inc=(k == nk - 1 and d == tiles[-1]), skip=True)
            return tok

        gb_free = {"s": [None] * 3, "h": [None] * 3}

        def glu(src, nunits, rhs, gsil, ghid, scale=None, *toks):
            pend = []
            state = {"last": None}

            def down(f, h, th, un, w, last):
                for d in range(8):
                    off = 4096 + (f % 2) * 1024 + d * 128
                    tok = mm(acc_tile(d), w[:, off:off + 128], h, f == 0 and d % 2 == 0, last,
                             th, acc_free[0], inc=(d == 7), skip=True)
                gb_free["h"][f % 3] = tok
                if f % 2:
                    release(un, tok)
                state["last"] = tok

            for u in range(nunits):
                un, w, tw = unit(src[u], UNIT)
                w3 = w[:, 0:4096].rearrange("p (a k n) -> p a k n", a=2, k=8)
                for j in range(2):
                    f = 2 * u + j
                    i, b, free = bank()
                    for a in range(2):
                        for k in range(8):
                            tok = mm(b[:, a * T:(a + 1) * T], w3[:, a, k, j * 128:(j + 1) * 128], rhs(k), k == 0, k == 7,
                                     tw, free, *toks, inc=(a == 1 and k == 7))
                    s, h = gsil[:, f % 3, :], ghid[:, f % 3, :]
                    t1 = A_(s, b[:, 0:T], ACT.Silu, tok, gb_free["s"][f % 3])
                    t2 = tt(h, s, b[:, T:2 * T], MUL, t1, gb_free["h"][f % 3])
                    wk_free[i] = t2
                    gb_free["s"][f % 3] = t2
                    if scale is not None:
                        row, tr_ = scale(f)
                        t2 = tt(h, h, row, MUL, tr_)
                    pend.append((f, h, t2, un, w, f == 2 * nunits - 1))
                    if len(pend) > 1:
                        down(*pend.pop(0))
            down(*pend.pop(0))
            return state["last"]

        class Scr:
            def __init__(self):
                self.at = 0

            def get(self, *shape):
                n = int(np.prod(shape))
                ap = scr[:, self.at:self.at + n]
                self.at += n
                assert self.at <= 18000, self.at
                if len(shape) == 2:
                    ap = ap.rearrange("p (a b) -> p a b", a=shape[0])
                elif len(shape) == 3:
                    ap = ap.rearrange("p (a b c) -> p a b c", a=shape[0], b=shape[1])
                return ap

        def softmax_rows(S, st, *toks, src=None):
            src = S if src is None else src
            t = red(st[:, 0, :], src, MAX, *toks, negate=True)
            for q in range(2):
                t = A_(S[:, q, :], src[:, q, :], ACT.Exp, t, bias=st[:, 0, q:q + 1], accum_out=st[:, 1, q:q + 1])
            return recip(st[:, 2, :], st[:, 1, :], t)

        def transpose_p(P, pT, *toks, free_pT=None):
            i, b, free = bank()
            for kt in range(2):
                for q in range(2):
                    t = tr(b[:, kt * T + q * 128:kt * T + (q + 1) * 128], P[:, q, kt * 128:(kt + 1) * 128],
                           *toks, free, inc=(kt == 1 and q == 1))
            t2 = A_(pT, b[:, :].rearrange("p (a b) -> p a b", a=2), ACT.Copy, t, free_pT)
            wk_free[i] = t2
            return t, t2

        S1 = Scr()
        mix = S1.get(8, T)
        vtm = S1.get(2, 768)
        mh = S1.get(8, T)
        base_at = S1.at
        qz = S1.get(4, T)
        kinv = S1.get(2, T)
        kendT = S1.get(2, T)
        kend = S1.get(2, 2, 128)
        rsil = S1.get(4, T)
        ATm = S1.get(4, 2, 128)
        Sst = S1.get(3, 2 * T)
        cum = S1.get(2, T)
        gl = S1.get(2, T)
        expP = S1.get(2, T)
        expN = S1.get(2, T)
        expE = S1.get(2, T)
        lrT = S1.get(T)
        S1b = Scr()
        S1b.at = base_at
        mqz = S1b.get(4, T)
        mk = S1b.get(2, T)
        vz = S1b.get(2, 4, 128)
        Sb = [S1b.get(2, T) for _ in range(3)]
        pT = [S1b.get(2, T) for _ in range(2)]
        st = [S1b.get(3, 2) for _ in range(3)]
        mbias = S1b.get(4, 2 * T)

        memx = hT
        t_mem = load(memx[:, :, :], A["memT"].rearrange("(k p) t -> p k t", p=128))

        z0 = memset(qz, 0.0)
        z1 = memset(ATm, 0.0)
        t_mh = norm_in(mh, memx, sm("mem_g"), t_mem)
        t_h = norm_in(hT, xT, sm("attn_g"), t_x)

        un, w, tw = unit(A["u_in0"], 8 * 528)
        w0 = w.rearrange("p (k n) -> p k n", k=8)
        i, b, free = bank()
        for k in range(8):
            tok = mm(b[0:16, 0:T], w0[:, k, 512:528], hT[:, k, :], k == 0, k == 7, tw, t_h, free, inc=(k == 7))
        t_lr = A_(lrT[0:16, :], b[0:16, 0:T], ACT.Copy, tok)
        wk_free[i] = t_lr
        i, b, free = bank()
        for j in range(2):
            tok = mm(b[:, j * T:(j + 1) * T], sm("w_gk")[0:16, j * 128:(j + 1) * 128], lrT[0:16, :], True, True,
                     t_lr, free, inc=(j == 1))
        for j in range(2):
            bj = b[:, j * T:(j + 1) * T]
            t = ts(cum[:, j, :], bj, sm("b_gk", j, j + 1), 0.0, ADD, MIN, tok)
        for j in range(2):
            t2 = A_(gl[:, j, :], b[:, j * T:(j + 1) * T], ACT.Abs, t, bias=sm("b_gk", j, j + 1))
        wk_free[i] = t2
        t2 = A_(gl, gl, ACT.Exp, scale=-1.0)
        t2 = A_(gl, gl, ACT.Ln, bias=1.0)
        t = tt(gl, cum, gl, SUB, t2)
        for j in range(2):
            t = dve.do(lambda e, j=j: e.tensor_tensor_scan(cum[:, j, :], cs("scanm"), gl[:, j, :], 0.0, MUL, ADD),
                       dve.last)
        A_(expP, cum, ACT.Exp, t, scale=1.0 / 16)
        t_n = A_(expN, cum, ACT.Exp, t, scale=-1.0 / 16)
        cl = cum.rearrange("p a (c t) -> p (a c) t", t=64)
        t = tt(gl.rearrange("p a (c t) -> p (a c) t", t=64), cl, cl[:, :, 63:64].broadcast_to([128, 8, 64]), SUB)
        t_e = A_(expE, gl, ACT.Exp, t, scale=-1.0 / 16)

        def q_evac(i0, n, b, tok):
            for j in range(2):
                for o in range(2):
                    p = slice(64 * o, 64 * o + 64)
                    t = stt(qz[p, 2 * j + o, :], b[p, j * T:(j + 1) * T], 0.125, expP[p, j, :], MUL, MUL, tok, t_n, z0)
            return t

        def k_evac(i0, n, b, tok):
            b3 = b[:, :].rearrange("p (a t) -> p a t", a=2)
            tt(kinv, b3, expN, MUL, tok, t_n)
            return tt(kendT, b3, expE, MUL, t_e)

        lin_fm(lambda k, i: w0[:, k, i * 128:(i + 1) * 128], 8, lambda k: hT[:, k, :], 2, q_evac, tw)
        t_q = dve.last
        lin_fm(lambda k, i: w0[:, k, 256 + i * 128:256 + (i + 1) * 128], 8, lambda k: hT[:, k, :], 2, k_evac, tw)
        t_k = dve.last
        release(un, pe.last)

        un, w, tw = unit(A["u_in1"], 8 * 768)
        w1 = w.rearrange("p (k n) -> p k n", k=8)
        for tt_ in range(2):
            for (a, n) in ((0, 512), (512, 256)):
                i, b, free = bank()
                for k in range(8):
                    tok = mm(b[:, 0:n], hT[:, k, tt_ * 128:(tt_ + 1) * 128], w1[:, k, a:a + n], k == 0, k == 7,
                             tw, free, inc=(k == 7))
                wk_free[i] = A_(vtm[:, tt_, a:a + n], b[:, 0:n], ACT.Copy, tok)
        t_v = act.last
        release(un, pe.last)

        for bb in range(2):
            i, b, free = bank()
            for h in range(4):
                tok = mm(b[:, h * 128:(h + 1) * 128], kinv[:, h // 2, bb * 128:(bb + 1) * 128],
                         qz[:, h, bb * 128:(bb + 1) * 128], True, True, t_q, t_k, free, inc=(h == 3))
            mk_ = cs("mask").bitcast(U32).rearrange("p (o t) -> p o t", o=1).broadcast_to([128, 4, 128])
            t = dve.do(lambda e, b=b, bb=bb, mk_=mk_: e.copy_predicated(
                ATm[:, :, bb, :], mk_, b[:, :].rearrange("p (h t) -> p h t", h=4)), tok, z1, dve.last)
            wk_free[i] = t
        t_A = dve.last
        i, b, free = bank()
        for bb in range(2):
            for p in range(2):
                tok = tr(b[:, (bb * 2 + p) * 128:(bb * 2 + p + 1) * 128], kendT[:, p, bb * 128:(bb + 1) * 128], t_k, free,
                         inc=(bb == 1 and p == 1))
        t_ke = A_(kend, b[:, :].rearrange("p (a b c) -> p a b c", a=2, b=2), ACT.Copy, tok)
        wk_free[i] = t_ke
        dS = []
        for n in range(3):
            i, b, free = bank()
            r = slice(64 * (n % 2), 64 * (n % 2) + 64)
            for p in range(2):
                tok = mm(b[:, p * T:(p + 1) * T], kend[r, n // 2, p, :], vtm[r, n // 2, p * T:(p + 1) * T], True, True,
                         t_ke, t_v, free, inc=(p == 1))
            if n == 0:
                t = cp(Sst[:, 0, :], b[:, :], tok)
            else:
                for p in range(2):
                    t = stt(Sst[:, n, p * T:(p + 1) * T], Sst[:, n - 1, p * T:(p + 1) * T],
                            expP[:, p, 64 * n + 63:64 * n + 64], b[:, p * T:(p + 1) * T], MUL, ADD, tok)
            wk_free[i] = t
        t_S = dve.last
        for h in range(4):
            p = h // 2
            o = acc[:, p, (h % 2) * T:(h % 2 + 1) * T]
            for bb in range(2):
                mm(o[:, bb * 128:(bb + 1) * 128], vtm[:, bb, h * 128:(h + 1) * 128], ATm[:, h, bb, :],
                   h % 2 == 0 and bb == 0, False, t_A, t_v, skip=True)
            for n in range(1, 4):
                tok = mm(o[:, n * 64:(n + 1) * 64], Sst[:, n - 1, p * T + (h % 2) * 128:p * T + (h % 2 + 1) * 128],
                         qz[:, h, n * 64:(n + 1) * 64], False, True, t_S, inc=(n == 3), skip=True)
        t_o = tok

        un, w, tw = unit(A["u_in2"], 8 * 512)
        w2 = w.rearrange("p (k n) -> p k n", k=8)

        def r_evac(i0, n, b, tok):
            return A_(rsil[:, i0:i0 + n, :], b[:, :].rearrange("p (a t) -> p a t", a=2), ACT.Silu, tok)

        lin_fm(lambda k, i: w2[:, k, i * 128:(i + 1) * 128], 8, lambda k: hT[:, k, :], 4, r_evac, tw)
        t_r = act.last
        release(un, pe.last)

        o3 = acc3[:, 0:4, :]
        for p in range(2):
            rs, t, r = stat(o3[:, 2 * p:2 * p + 2, :], cs("ones128"), 2, [[0], [1]], t_o)
            for j in range(2):
                h = 2 * p + j
                stt(mix[:, h, :], o3[:, h, :], sm("gla_g"), rs[j], MUL, MUL, t)
                t2 = tt(mix[:, h, :], mix[:, h, :], rsil[:, h, :], MUL, t_r)
            rs_free[r] = t2
        acc_free[0] = dve.last
        t_gla = dve.last
        fence()

        t_mb = load(mbias, A["mbias"], dve.last, act.last, pe.last)
        z0 = memset(mqz, 0.0)
        z2 = memset(vz, 0.0)
        un, w, tw = unit(A["u_in3"], 8 * 768)
        w3_ = w.rearrange("p (k n) -> p k n", k=8)

        def normed(col, gname, dst_z, dst_f, rhs, wv, tw, z=None):
            def ev(i0, n, b, tok):
                b3 = b[:, :].rearrange("p (a t) -> p a t", a=2)
                rs, t, r = stat(b3, cs("onesB"), 2, [[0], [1]], tok)
                for j in range(2):
                    if dst_f is not None:
                        t2 = stt(dst_f[:, j, :], b3[:, j, :], sm(gname), rs[j], MUL, MUL, t)
                    else:
                        for o in range(2):
                            p = slice(64 * o, 64 * o + 64)
                            t2 = stt(dst_z[p, 2 * j + o, :], b3[p, j, :], sm(gname)[p, :], rs[j][p, :], MUL, MUL, t, z)
                rs_free[r] = t2
                return t2
            lin_fm(lambda k, i: wv[:, k, col + i * 128:col + (i + 1) * 128], 8, rhs, 2, ev, tw)
            return dve.last

        def attend(qzt, kf, vzt, bias, first, t_in):
            for pr in range(2):
                bo, freeo = acc[:, pr, :], acc_free[0]
                for j in range(2):
                    h = 2 * pr + j
                    i, b, free = bank()
                    for q in range(2):
                        tok = mm(b[:, q * T:(q + 1) * T], qzt[:, h, q * 128:(q + 1) * 128], kf[:, h // 2, :], True, True,
                                 t_in, free, inc=(q == 1))
                    S, s_ = Sb[h % 3], st[h % 3]
                    b3 = b[:, :].rearrange("p (a t) -> p a t", a=2)
                    if bias is not None:
                        t = stt(S, b3, 0.125, bias[:, h, :].rearrange("p (a t) -> p a t", a=2), MUL, ADD, tok, t_mb, pe.last)
                    else:
                        t = ts(S, b3, 0.125, None, MUL, None, tok, pe.last)
                    wk_free[i] = t
                    t = softmax_rows(S, s_, t)
                    for q in range(2):
                        t = ts(S[:, q, :], S[:, q, :], s_[:, 2, q:q + 1], None, MUL, None, t)
                    _, t = transpose_p(S, pT[h % 2], t, free_pT=pe.last)
                    for kt in range(2):
                        tok = mm(bo[:, 0:T], vzt[:, kt, h, :], pT[h % 2][:, kt, :], j == 0 and kt == 0,
                                 j == 1 and kt == 1, t, freeo, inc=(kt == 1))
                last = A_(mix[:, first + pr, :], bo[:, 0:T], ACT.Copy, tok)
            acc_free[0] = last

        normed(0, "mbq_g", mqz, None, lambda k: hT[:, k, :], w3_, tw, z0)
        t_k = normed(256, "mbk_g", None, mk, lambda k: hT[:, k, :], w3_, tw)
        for h in range(4):
            o = 64 * (h % 2)
            t = cp(vz[:, :, h, o:o + 64], vtm[:, :, 512 + h * 64:512 + h * 64 + 64], t_v, z2)
        attend(mqz, mk, vz, mbias, 4, t)
        t_mz = memset(mqz, 0.0, pe.last)
        normed(512, "mq_g", mqz, None, lambda k: hT[:, k, :], w3_, tw, t_mz)
        release(un, pe.last)
        un, w, tw = unit(A["u_mem"], 8 * 512)
        w4 = w.rearrange("p (k n) -> p k n", k=8)
        dve.wait(pe.last)
        normed(0, "mk_g", None, mk, lambda k: mh[:, k, :], w4, tw)
        for q in range(2):
            i, b, free = bank()
            for k in range(8):
                tok = mm(b[:, 0:256], mh[:, k, q * 128:(q + 1) * 128], w4[:, k, 256:512], k == 0, k == 7, tw, free, inc=(k == 7))
            for h in range(4):
                o = 64 * (h % 2)
                t = cp(vz[:, q, h, o:o + 64], b[:, h * 64:h * 64 + 64], tok)
            wk_free[i] = t
        release(un, pe.last)
        attend(mqz, mk, vz, None, 6, dve.last)
        t_mix = act.last

        for half in range(2):
            un, w, tw = unit(A["u_out"][half], 8 * 512)
            wo = w.rearrange("p (k n) -> p k n", k=8)
            tok = lin_acc(8, lambda k, d: wo[:, k, (d % 4) * 128:(d % 4 + 1) * 128], lambda k: mix[:, k, :],
                          tw, t_mix, tiles=range(4 * half, 4 * half + 4))
            release(un, tok)
        t = tt(xT[:, :, :], xT[:, :, :], acc3, ADD, tok)
        acc_free[0] = t

        def finish(src=xT):
            s = sem("s_fin")
            act.wait(dve.last, act.last)
            act.q.append(lambda e: e.dma_start(out.rearrange("(k p) t -> p k t", p=128), src[:, :, :]).then_inc(s, 16))
            act.q.append(lambda e: e.wait_ge(s, 16))

        def emit():
            block = ctx.enter_context(nc.Block())

            @block.sync
            def _(e):
                for n, (src, ncols) in enumerate(units):
                    if n >= NSLOT:
                        e.wait_ge(*released[n - NSLOT])
                    e.dma_start(ring[:, n % NSLOT, 0:ncols], src).then_inc(s_ring[n % NSLOT], 16)

            def play(g):
                def body(e):
                    for f in g.q:
                        f(e)
                return body

            block.tensor(play(pe))
            block.vector(play(dve))
            block.scalar(play(act))
            block.gpsimd(play(pool))

        if stage == 0:
            finish(mix)
            return emit()
        if stage == 1:
            finish()
            return emit()

        fence()
        S2 = Scr()
        gsil = S2.get(3, T)
        ghid = S2.get(3, T)
        L = S2.get(2, 36)
        R = S2.get(2, 96)
        comb = S2.get(2, 32)
        combT = S2.get(T)
        sel = S2.get(32, 128)
        cb = S2.get(2, T)
        t_h = norm_in(hT, xT, sm("ffn_g"))
        wr = sm("w_r").rearrange("p (k n) -> p k n", k=8)
        i, b, free = bank()
        for q in range(2):
            for k in range(8):
                tok = mm(b[:, q * 36:(q + 1) * 36], hT[:, k, q * 128:(q + 1) * 128], wr[:, k, :], k == 0, k == 7, t_h,
                         free, inc=(k == 7 and q == 1))
        rb = sm("rbias").rearrange("p (o t) -> p o t", o=1).broadcast_to([128, 2, 36])
        t = tt(L, b[:, 0:72].rearrange("p (a n) -> p a n", a=2), rb, ADD, tok)
        wk_free[i] = t

        def onehot(dst, src, mx, n):
            tt(dst, src, mx.broadcast_to([128, 2, n]), ALU.is_ge)
            tw_ = cs("tiew").rearrange("p (o t) -> p o t", o=1)[:, :, 0:n].broadcast_to([128, 2, n])
            tt(dst, dst, tw_, MUL)
            m = R[:, :, 95:96]
            red(m, dst, MAX)
            return tt(dst, dst, m.broadcast_to([128, 2, n]), ALU.is_equal)

        gm, goh, gex, gsum = R[:, :, 0:1], R[:, :, 1:5], R[:, :, 5:9], R[:, :, 9:10]
        les, m1, oh1, les2, m2, oh2 = R[:, :, 10:18], R[:, :, 18:19], R[:, :, 19:27], R[:, :, 27:35], R[:, :, 35:36], R[:, :, 36:44]
        e2, p1, p2, c8 = R[:, :, 44:45], R[:, :, 45:46], R[:, :, 46:47], R[:, :, 48:56]
        red(gm, L[:, :, 0:4], MAX)
        onehot(goh, L[:, :, 0:4], gm, 4)
        t = tt(gex, L[:, :, 0:4], gm.broadcast_to([128, 2, 4]), SUB)
        t = A_(gex, gex, ACT.Exp, t)
        red(gsum, gex, ADD, t)
        for g in range(4):
            src = L[:, :, 4 + 8 * g:12 + 8 * g]
            oh = goh[:, :, g:g + 1].broadcast_to([128, 2, 8])
            if g == 0:
                tt(les, src, oh, MUL)
            else:
                tt(les2, src, oh, MUL)
                tt(les, les, les2, ADD)
        red(m1, les, MAX)
        onehot(oh1, les, m1, 8)
        ts(les2, oh1, -3e38, None, MUL, None)
        tt(les2, les2, les, ADD)
        red(m2, les2, MAX)
        onehot(oh2, les2, m2, 8)
        t = tt(e2, m2, m1, SUB)
        t = A_(e2, e2, ACT.Exp, t)
        ts(p1, e2, 1.0, None, ADD, None, t)
        tt(p1, p1, gsum, MUL)
        recip(p1, p1)
        tt(p2, p1, e2, MUL)
        tt(oh1, oh1, p1.broadcast_to([128, 2, 8]), MUL)
        tt(oh2, oh2, p2.broadcast_to([128, 2, 8]), MUL)
        tt(c8, oh1, oh2, ADD)
        for g in range(4):
            t = tt(comb[:, :, 8 * g:8 * g + 8], c8, goh[:, :, g:g + 1].broadcast_to([128, 2, 8]), MUL)
        i, b, free = bank()
        for q in range(2):
            tok = tr(b[0:32, q * 128:(q + 1) * 128], comb[:, q, :], t, free, inc=(q == 1))
        t_cT = cp(combT[0:32, :], b[0:32, 0:T], tok)
        wk_free[i] = t_cT
        t_sel = cp(sel[0:32, :, :], cs("ident", 0, 32)[0:32, :].rearrange("p (a o) -> p a o", o=1).broadcast_to([32, 32, 128]))

        row = {}
        cb_free = [None, None]

        def expert_row(f):
            e_ = f // 4
            if e_ not in row:
                i, b, free = bank()
                tok = mm(b[:, 0:T], sel[0:32, e_, :], combT[0:32, :], True, True, t_sel, t_cT, free, inc=True)
                t = A_(cb[:, e_ % 2, :], b[:, 0:T], ACT.Copy, tok, cb_free[e_ % 2])
                wk_free[i] = t
                row[e_] = t
            if f % 4 == 3:
                cb_free[e_ % 2] = (dve.sem, dve.n + 1)
            return cb[:, e_ % 2, :], row[e_]

        tok = glu([A["u_moe"][u] for u in range(64)], 64, lambda k: hT[:, k, :], gsil, ghid, expert_row, t_h)
        t = tt(xT[:, :, :], xT[:, :, :], acc3, ADD, tok)
        acc_free[0] = t
        if stage == 2:
            finish()
            return emit()

        def ffn(i, j):
            g = 2 * j * 2
            a = (i * 8 + g) * 8
            t_h = norm_in(hT, xT, sm("norm_g", a, a + 8))
            tok = glu([A["u_ffn"][(2 * i + j) * 11 + u] for u in range(11)], 11, lambda k: hT[:, k, :], gsil, ghid, None, t_h)
            return norm_add(acc3, sm("norm_g", a + 8, a + 16), tok, half=True)

        def ng(i, g):
            return sm("norm_g", (i * 8 + g) * 8, (i * 8 + g + 1) * 8)

        def ple(i):
            fence()
            S = Scr()
            S.at = 1536
            pTt = S.get(2, T)
            sg = S.get(8, T)
            t_p = load(pTt, A["pT"][i].rearrange("(k p) t -> p k t", p=128), pe.last, act.last, dve.last)
            t_h = norm_in(hT, xT, ng(i, 6))
            for half in range(2):
                un, w, tw = unit(A["u_ple"][2 * i + half], 5120)
                wg = w[:, 0:4096].rearrange("p (k n) -> p k n", k=8)
                wp = w[:, 4096:5120].rearrange("p (k n) -> p k n", k=2)

                def ev(i0, n, b, tok):
                    return A_(sg[:, 4 * half + i0:4 * half + i0 + 2, :], b[:, :].rearrange("p (a t) -> p a t", a=2), ACT.Sigmoid, tok)

                lin_fm(lambda k, c: wg[:, k, c * 128:(c + 1) * 128], 8, lambda k: hT[:, k, :], 4, ev, tw, t_h)
                tok = lin_acc(2, lambda k, d: wp[:, k, (d % 4) * 128:(d % 4 + 1) * 128], lambda k: pTt[:, k, :],
                              tw, t_p, tiles=range(4 * half, 4 * half + 4))
                release(un, tok)
            t = tt(sg, sg, acc3, MUL, tok, act.last)
            acc_free[0] = t
            rs, t, r = stat(sg, cs("onesD"), 8, [list(range(8))], t)
            g = ng(i, 7)
            for k in range(8):
                t2 = stt(hT[:, k, :], sg[:, k, :], g[:, k:k + 1], rs[0], MUL, MUL, t, pe.last)
            rs_free[r] = t2
            return tt(xT[:, :, :], xT[:, :, :], hT[:, :, :], ADD, t2)

        ffn(0, 0)
        fence()
        S3 = Scr()
        S3.at = 1536
        qz2 = S3.get(16, T)
        kf = S3.get(8, T)
        V = S3.get(2, 1024)
        o2 = S3.get(8, T)
        Sb2 = [S3.get(2, T) for _ in range(3)]
        aT = [S3.get(2, T) for _ in range(2)]
        bt = [S3.get(2, 384) for _ in range(2)]
        st2 = [S3.get(3, 2) for _ in range(3)]
        lam = S3.get(8)
        lm = [S3.get(2), S3.get(2)]
        rvec = S3.get(512)
        lamt = S3.get(2, 64)
        t_h = norm_in(hT, xT, ng(0, 2))
        i, b, free = bank()
        tok = mm(b[0:16, :], sm("relb")[0:32, :], cs("bucket")[0:32, :], True, True, free, inc=True)
        t = tt(rvec[0:16, :], b[0:16, :], cs("cut")[0:16, :], ADD, tok)
        wk_free[i] = t
        s_rv = sem("s_rv")
        act.wait(t)
        rdram = A["rscratch"]
        act.q.append(lambda e: e.dma_start(rdram, rvec[0:16, :]).then_inc(s_rv, 16))
        lv = sm("lamv").rearrange("p (a b n) -> p a b n", a=2, b=2)
        tt(lamt, lv[:, :, 0, :], lv[:, :, 1, :], MUL)
        t = red(lam[:, 0:2], lamt, ADD)
        t = A_(lam[:, 2:4], lam[:, 0:2], ACT.Exp, t)
        tt(lam[:, 4:5], lam[:, 2:3], lam[:, 3:4], SUB, t)
        ts(lam[:, 4:5], lam[:, 4:5], 0.8 - 0.6 * math.exp(0.0), None, ADD, None)
        z = memset(qz2, 0.0)
        tiles = []
        for u, ncol in ((0, 768), (1, 768), (2, 512)):
            un, w, tw = unit(A[f"u_qk{u}"], 8 * ncol)
            wq = w.rearrange("p (k n) -> p k n", k=8)
            base = [0, 6, 12][u]

            def ev(i0, n, b, tok):
                c = base + i0
                b3 = b[:, :].rearrange("p (a t) -> p a t", a=2)
                if c >= 8:
                    return A_(kf[:, c - 8:c - 6, :], b3, ACT.Copy, tok)
                q4 = qz2[:, 2 * c:2 * c + 4, :].rearrange("p (a m) t -> p a m t", m=2)
                A_(q4[0:64, :, 0, :], b3[0:64, :, :], ACT.Copy, tok, z, scale=0.125)
                return A_(q4[64:128, :, 1, :], b3[64:128, :, :], ACT.Copy, tok, scale=0.125)

            lin_fm(lambda k, c: wq[:, k, c * 128:(c + 1) * 128], 8, lambda k: hT[:, k, :], ncol // 128, ev, tw, t_h)
            release(un, pe.last)
        for half in range(2):
            un, w, tw = unit(A["u_v"][half], 8 * 512)
            wv = w.rearrange("p (k n) -> p k n", k=8)
            for q in range(2):
                i, b, free = bank()
                for k in range(8):
                    tok = mm(b[:, :], hT[:, k, q * 128:(q + 1) * 128], wv[:, k, :], k == 0, k == 7, tw, free, inc=(k == 7))
                wk_free[i] = cp(V[:, q, half * 512:(half + 1) * 512], b[:, :], tok)
            release(un, tok)
        t_qkv = [act.last, dve.last]
        bt_free = [None, None]
        aT_free = [None, None]
        for h in range(8):
            bh = bt[h % 2]
            act.wait(bt_free[h % 2], (s_rv, 16))
            sbt = []
            for m in range(2):
                src = bass.AP(tensor=rdram.tensor, offset=rdram.offset + (2 * h + m) * 512,
                              ap=[[1, 128], [1, 384]])
                sbt.append(load(bh[:, m, :], src))
            Ss = []
            for m in range(2):
                c = 2 * h + m
                i, b, free = bank()
                for q in range(2):
                    mm(b[:, q * T:(q + 1) * T], qz2[:, c, q * 128:(q + 1) * 128], kf[:, h, :], True, False,
                       *t_qkv, free)
                    tok = mm(b[:, q * T:(q + 1) * T], cs("anti"), bh[:, m, 128 - 128 * q:384 - 128 * q], False, True,
                             sbt[m], inc=(q == 1))
                bt_free[h % 2] = tok
                S, s_ = Sb2[c % 3], st2[c % 3]
                t = softmax_rows(S, s_, tok, src=b[:, :].rearrange("p (a t) -> p a t", a=2))
                wk_free[i] = act.last
                Ss.append((S, s_))
            (P0, r0), (P1, r1) = Ss
            lmh = lm[h % 2]
            t = ts(lmh, r1[:, 2, :], lam[:, 4:5], None, MUL, None, t)
            for q in range(2):
                ts(P1[:, q, :], P1[:, q, :], lmh[:, q:q + 1], None, MUL, None)
                t = stt(P0[:, q, :], P0[:, q, :], r0[:, 2, q:q + 1], P1[:, q, :], MUL, SUB)
            _, t = transpose_p(P0, aT[h % 2], t, free_pT=aT_free[h % 2])
            i, b, free = bank()
            for kt in range(2):
                tok = mm(b[:, 0:T], V[:, kt, h * 128:(h + 1) * 128], aT[h % 2][:, kt, :], kt == 0, kt == 1, t, free, inc=(kt == 1))
            aT_free[h % 2] = tok
            wk_free[i] = A_(o2[:, h, :], b[:, 0:T], ACT.Copy, tok)
        ts(sm("subln_g"), sm("subln_g"), 1.0 - (0.8 - 0.6), None, MUL, None)
        for p in range(4):
            rs, t, r = stat(o2[:, 2 * p:2 * p + 2, :], cs("ones128"), 2, [[0], [1]])
            for j in range(2):
                t2 = stt(o2[:, 2 * p + j, :], o2[:, 2 * p + j, :], sm("subln_g"), rs[j], MUL, MUL, t)
            rs_free[r] = t2
        t_o2 = dve.last
        for half in range(2):
            un, w, tw = unit(A["u_o"][half], 8 * 512)
            wo = w.rearrange("p (k n) -> p k n", k=8)
            tok = lin_acc(8, lambda k, d: wo[:, k, (d % 4) * 128:(d % 4 + 1) * 128], lambda k: o2[:, k, :],
                          tw, t_o2, tiles=range(4 * half, 4 * half + 4))
            release(un, tok)
        if stage == 3:
            cp(xT[:, :, :], acc3, tok)
            finish()
            return emit()
        norm_add(acc3, ng(0, 3), tok)
        ffn(0, 1)
        ple(0)
        ffn(1, 0)
        if stage == 4:
            finish()
            return emit()

        fence()
        S4 = Scr()
        S4.at = 1536
        r_ = S4.get(32)
        phi = S4.get(32)
        wre, wim = S4.get(32), S4.get(32)
        tA, tB, tC, tE = S4.get(32), S4.get(32), S4.get(32), S4.get(32)
        Bre, Bim = S4.get(8, 128), S4.get(8, 128)
        Cre, Cim, Cx, Cy = S4.get(32, 32), S4.get(32, 32), S4.get(32, 32), S4.get(32, 32)
        t_B = [load(x, A[n], dve.last, act.last, pe.last) for x, n in ((Bre, "sBre"), (Bim, "sBim"), (Cx, "sCre"), (Cy, "sCim"))]
        th = S4.get(T)
        sn = [S4.get(T) for _ in range(2)]
        co = [S4.get(T) for _ in range(2)]
        nn = S4.get(T)
        pr = [S4.get(2, T) for _ in range(2)]
        pq = S4.get(2, T)
        ww = [S4.get(2, T) for _ in range(2)]
        md = [S4.get(4, T) for _ in range(2)]
        t_h = norm_in(hT, xT, ng(1, 2))

        t = A_(tA, sm("log_dt"), ACT.Exp)
        tt(tB, sm("lam_re"), tA, MUL, t)
        t = tt(tC, sm("lam_im"), tA, MUL)
        t = A_(r_, tB, ACT.Exp, t)
        ts(phi, tC, 1.0 / TWO_PI, None, MUL, None)

        def frac(dst, src, tmp):
            ts(tmp, src, MAGIC, None, ADD, None)
            ts(tmp, tmp, MAGIC, None, SUB, None)
            return tt(dst, src, tmp, SUB)

        def sincos(s_out, c_out, f, tmp, *toks):
            A_(s_out, f, ACT.Sin, *toks, scale=TWO_PI * (1 - 1e-7))
            A_(tmp, f, ACT.Abs)
            return A_(c_out, tmp, ACT.Sin, scale=-TWO_PI, bias=cs("halfpi"))

        t = frac(tE, phi, wre)
        t = sincos(tC, tB, tE, wim, t)
        ta = tt(tB, r_, tB, MUL, t)
        tt(tC, r_, tC, MUL)
        ts(tB, tB, -1.0, None, ADD, None)
        lr, li = sm("lam_re"), sm("lam_im")
        tt(tA, lr, lr, MUL)
        tt(tE, li, li, MUL)
        tt(tA, tA, tE, ADD)
        recip(tA, tA)
        tt(wre, tB, lr, MUL)
        tt(tE, tC, li, MUL)
        tt(wre, wre, tE, ADD)
        tt(wre, wre, tA, MUL)
        tt(wim, tC, lr, MUL)
        tt(tE, tB, li, MUL)
        tt(wim, wim, tE, SUB)
        tt(wim, wim, tA, MUL)
        wr3 = wre.rearrange("p (a o) -> p a o", o=1).broadcast_to([128, 32, 32])
        wi3 = wim.rearrange("p (a o) -> p a o", o=1).broadcast_to([128, 32, 32])
        for tb in t_B:
            dve.wait(tb)
            pe.wait(tb)
        tt(Cre, Cx, wr3, MUL)
        tt(Cim, Cy, wi3, MUL)
        tt(Cre, Cre, Cim, SUB)
        tt(Cim, Cx, wi3, MUL)
        tt(Cx, Cy, wr3, MUL)
        tt(Cim, Cim, Cx, ADD)
        t_C = ts(Cy, Cim, -1.0, None, MUL, None)
        ts(Cx, Cre, -1.0, None, MUL, None)
        t_C = dve.last
        tab_free = [None, None]
        pr_free = [None, None]
        md_free = [None, None]
        for s in range(32):
            k, j = s // 4, s % 4
            x2 = s % 2
            i, b, free = bank()
            rr = slice(32 * j, 32 * j + 32)
            for a, Bt in enumerate((Bre, Bim)):
                tok = mm(b[:, a * T:(a + 1) * T], Bt[rr, k, :], hT[rr, k, :], True, True, t_h, free, inc=(a == 1))
            ph = phi[:, s:s + 1]
            ts(nn, cs("tvec"), ph, MAGIC, MUL, ADD)
            ts(nn, nn, MAGIC, None, SUB, None)
            t = stt(th, cs("tvec"), ph, nn, MUL, SUB, act.last)
            t = sincos(sn[x2], co[x2], th, pq[:, 0, :], t, tab_free[x2], dve.last)
            c1, s1 = co[x2], sn[x2]
            vr, vi = b[:, 0:T], b[:, T:2 * T]
            P, Q = pr[x2], ww[x2]
            tt(P[:, 0, :], vr, c1, MUL, tok, t)
            tt(Q[:, 0, :], vi, s1, MUL)
            tt(P[:, 0, :], P[:, 0, :], Q[:, 0, :], ADD)
            tt(P[:, 1, :], vi, c1, MUL)
            t = tt(Q[:, 1, :], vr, s1, MUL)
            wk_free[i] = t
            tt(P[:, 1, :], P[:, 1, :], Q[:, 1, :], SUB)
            rb_ = r_[:, s:s + 1].broadcast_to([128, T])
            for a in range(2):
                dve.do(lambda e, a=a, P=P, Q=Q, rb_=rb_: e.tensor_tensor_scan(Q[:, a, :], rb_, P[:, a, :], 0.0, MUL, ADD), dve.last)
            M = md[x2]
            dve.wait(md_free[x2])
            tt(M[:, 0, :], c1, Q[:, 0, :], MUL)
            tt(M[:, 1, :], s1, Q[:, 1, :], MUL)
            tt(M[:, 2, :], c1, Q[:, 1, :], MUL)
            t = tt(M[:, 3, :], s1, Q[:, 0, :], MUL)
            tab_free[x2] = t
            dst = acc[rr, k // 2, (k % 2) * T:(k % 2 + 1) * T]
            for a, Cc in enumerate((Cre, Cx, Cy, Cy)):
                tok = mm(dst, Cc[:, s, :], M[:, a, :], k % 2 == 0 and a == 0, a == 3, t, t_C, acc_free[0],
                         inc=(a == 3), skip=True)
            md_free[x2] = tok
        for k in range(8):
            t = stt(sq[:, k, :], hT[:, k, :], sm("ssm_d", k, k + 1), acc3[:, k, :], MUL, ADD, tok)
        acc_free[0] = t
        t_y = A_(hT[:, :, :], sq[:, :, :], ACT.Gelu_apprx_tanh, t)
        S5 = Scr()
        S5.at = 1536 + 512
        fence()
        zz = S5.get(8, T)
        zs = S5.get(2, T)
        for u in range(4):
            un, w, tw = unit(A["u_glu"][u], 4096)
            wg = w.rearrange("p (k n) -> p k n", k=8)
            banks = []

            def ev(i0, n, b, tok):
                banks.append(b)
                if i0 == 0:
                    return "busy"
                for j in range(2):
                    c = 2 * u + j
                    t = A_(zs[:, j, :], b[:, j * T:(j + 1) * T], ACT.Sigmoid, tok, bias=sm("b_glu", 8 + c, 9 + c))
                for j in range(2):
                    c = 2 * u + j
                    t2 = stt(zz[:, c, :], banks[0][:, j * T:(j + 1) * T], sm("b_glu", c, c + 1), zs[:, j, :], ADD, MUL, t)
                wk_free[(wk_at[0] - 2) % 4] = t2
                act.wait(t2)
                return t
            lin_fm(lambda k, c: wg[:, k, c * 128:(c + 1) * 128], 8, lambda k: hT[:, k, :], 4, ev, tw, t_y)
            release(un, pe.last)
        rs, t, r = stat(zz, cs("onesD"), 8, [list(range(8))], dve.last)
        g = ng(1, 3)
        if stage == 5:
            cp(xT[:, :, :], zz)
            finish()
            return emit()
        for k in range(8):
            t2 = stt(hT[:, k, :], zz[:, k, :], g[:, k:k + 1], rs[0], MUL, MUL, t, pe.last)
        rs_free[r] = t2
        tt(xT[:, :, :], xT[:, :, :], hT[:, :, :], ADD, t2)
        ffn(1, 1)
        ple(1)
        finish()
        return emit()


def _ktile(w, cols=None):
    K, N = w.shape
    return np.ascontiguousarray(w.reshape(K // 128, 128, N).transpose(1, 0, 2).reshape(128, -1))


def _glu_units(wg, wu, wd):
    n, _, F = wg.shape
    u = F // 256
    out = np.empty((n, u, 128, UNIT), wg.dtype)
    v = out[..., 0:4096].reshape(n, u, 128, 2, 8, 256)
    for a, w in enumerate((wg, wu)):
        v[:, :, :, a] = w.reshape(n, 8, 128, u, 256).transpose(0, 3, 2, 1, 4)
    out[..., 0:4096] = v.reshape(n, u, 128, 4096)
    out[..., 4096:] = wd.reshape(n, u, 2, 128, 1024).transpose(0, 1, 3, 2, 4).reshape(n, u, 128, 2048)
    return out.reshape(n * u, 128, UNIT)


def _feat(v):
    return v.reshape(-1, 8, 128).transpose(2, 0, 1).reshape(128, -1)


def _constants():
    c = np.zeros((128, NCC), np.float32)

    def put(name, v):
        a, b = CCOL[name]
        c[:, a:b] = v

    p = np.arange(128)
    put("ident", np.eye(128))
    put("anti", np.eye(128)[::-1])
    put("onesD", 1.0 / 1024)
    put("onesB", (p[:, None] // 64 == p[None, :] // 64) / 64.0)
    put("ones128", 1.0 / 128)
    put("mask", (p[:, None] // 64 == p[None, :] // 64) & (p[:, None] <= p[None, :]))
    put("tiew", 8.0 - np.arange(8))
    put("eps", 1e-6)
    put("halfpi", math.pi / 2)
    put("scanm", np.arange(256) % 64 != 0)
    put("tvec", np.arange(256))
    dist = 255 - np.arange(512)
    n = np.maximum(dist, 0)
    nf = np.maximum(n, 1).astype(np.float32)
    large = 16 + (np.log(nf / np.float32(16)) / np.float32(math.log(128 / 16)) * np.float32(16)).astype(np.int32)
    bucket = np.where(n < 16, n, np.minimum(large, 31))
    oh = np.zeros((128, 512), np.float32)
    oh[bucket, np.arange(512)] = 1.0
    oh[:, 511] = 0
    put("bucket", oh)
    put("cut", np.where(dist >= 0, 0.0, NEG)[None, :])
    slopes = (2.0 ** (-8.0 * np.arange(1, 5) / 4)).astype(np.float32)
    q = np.arange(256).reshape(2, 128).T
    d = (q[:, None, :, None] - np.arange(256)[None, None, None, :]).astype(np.float32)
    mb = np.where(d >= 0, -(slopes[None, :, None, None] * d), np.float32(NEG))
    return c, np.ascontiguousarray(mb.astype(np.float32).reshape(128, 4 * 512))


def _layout(i):
    f = {k: np.asarray(v) for k, v in i.items()}
    a = {}
    a["xT"] = np.ascontiguousarray(f["x"][0].T)
    a["memT"] = np.ascontiguousarray(f["mem"][0].T)
    w = f["w_in"][0]
    c = np.concatenate
    a["u_in0"] = _ktile(c([w[:, 0:512], w[:, 1536:1552]], 1))
    a["u_in1"] = _ktile(c([w[:, 512:1024], w[:, 2064:2320]], 1))
    a["u_in2"] = _ktile(w[:, 1024:1536])
    a["u_in3"] = _ktile(c([w[:, 1552:2064], w[:, 2320:2576]], 1))
    a["u_mem"] = _ktile(f["w_mem_kv"][0])
    a["u_out"] = np.stack([_ktile(f["w_out"][0][:, h * 512:(h + 1) * 512]) for h in range(2)])
    a["u_moe"] = _glu_units(f["w_gate"][0], f["w_up"][0], f["w_down"][0])
    fi = f["ffn_w_in_2"].reshape(4, 1024, 5632)
    a["u_ffn"] = _glu_units(fi[:, :, :2816], fi[:, :, 2816:], f["ffn_w_out_2"].reshape(4, 2816, 1024))
    qkv = f["attn_w_qkv_2"][0]
    for u, (s, e) in enumerate(((0, 768), (768, 1536), (1536, 2048))):
        a[f"u_qk{u}"] = _ktile(qkv[:, s:e])
    a["u_v"] = np.stack([_ktile(qkv[:, 2048 + h * 512:2560 + h * 512]) for h in range(2)])
    a["u_o"] = np.stack([_ktile(f["attn_w_o_2"][0][:, h * 512:(h + 1) * 512]) for h in range(2)])
    wg = f["ssm_w_glu_2"][0]
    a["u_glu"] = np.stack([_ktile(c([wg[:, u * 256:(u + 1) * 256], wg[:, 1024 + u * 256:1280 + u * 256]], 1)) for u in range(4)])
    a["u_ple"] = np.stack([c([_ktile(f["ple_w_gate_2"][i][:, h * 512:(h + 1) * 512]),
                              _ktile(f["ple_w_proj_2"][i][:, h * 512:(h + 1) * 512])], 1)
                           for i in range(2) for h in range(2)])
    a["pT"] = np.ascontiguousarray(f["p_2"][:, 0].transpose(0, 2, 1))
    s = np.zeros((128, NSC), np.float32)

    def put(name, v):
        x, y = SCOL[name]
        s[0:v.shape[0], x:y] = v

    put("attn_g", _feat(f["attn_norm_g"]))
    put("mem_g", _feat(f["mem_norm_g"]))
    put("ffn_g", _feat(f["ffn_norm_g"]))
    put("b_gk", f["b_gla_gk"].reshape(2, 128).T)
    put("gla_g", f["gla_out_norm_g"].T)
    for n, k in (("mbq_g", "moba_q_norm_g"), ("mbk_g", "moba_k_norm_g"), ("mq_g", "mem_q_norm_g"), ("mk_g", "mem_k_norm_g")):
        put(n, c([f[k].T, f[k].T], 0))
    put("norm_g", _feat(f["norm_g_2"]))
    put("subln_g", f["attn_subln_g_2"].T)

    def states(v):
        return v.reshape(32, 128).T

    put("lam_re", states(f["ssm_lam_re_2"][0]))
    put("lam_im", states(f["ssm_lam_im_2"][0]))
    put("log_dt", states(np.repeat(f["ssm_log_dt_2"][0][:, None], 64, 1)))
    put("ssm_d", _feat(f["ssm_d_2"]))
    put("b_glu", f["ssm_b_glu_2"].reshape(16, 128).T)
    put("lamv", np.broadcast_to(f["attn_lam_2"].reshape(1, 256), (128, 256)))
    put("rbias", np.broadcast_to(c([f["b_router_group"], f["b_router_expert"].reshape(1, 32)], 1), (128, 36)))
    wr = c([f["w_router_group"][0], f["w_router_expert"][0].transpose(1, 0, 2).reshape(1024, 32)], 1)
    put("w_r", _ktile(wr))
    put("w_gk", f["w_gla_gk"][0])
    put("relb", f["rel_bias_2"])
    a["small"] = s
    for n, k in (("sBre", "ssm_b_re_2"), ("sBim", "ssm_b_im_2")):
        v = np.zeros((8, 4, 2, 16, 2, 64), np.float32)
        src = f[k][0].reshape(8, 4, 2, 64, 16).transpose(0, 1, 2, 4, 3)
        for g in range(2):
            v[:, :, g, :, g, :] = src[:, :, g]
        a[n] = np.ascontiguousarray(v.reshape(8, 128, 128).transpose(1, 0, 2).reshape(128, 1024))
    for n, k in (("sCre", "ssm_c_re_2"), ("sCim", "ssm_c_im_2")):
        v = np.zeros((32, 2, 64, 2, 16), np.float32)
        src = f[k][0].reshape(32, 2, 16, 64).transpose(0, 1, 3, 2)
        for g in range(2):
            v[:, g, :, g, :] = src[:, g]
        a[n] = np.ascontiguousarray(v.reshape(32, 128, 32).transpose(1, 0, 2).reshape(128, 1024))
    a["cst"], a["mbias"] = _constants()
    return a


STAGE = 9


def kernel(**inputs):
    import numpy as _np
    import concourse.bacc as _bacc
    from concourse import mybir as _mybir
    from concourse.bass_utils import run_bass_kernel_spmd as _run

    nc = _bacc.Bacc("TRN2", target_bir_lowering=False, num_devices=1)
    lay = _layout(inputs)
    arrays, A = {}, {}
    for name, a in lay.items():
        arrays[f"in_{name}"] = a
        A[name] = nc.dram_tensor(f"in_{name}", a.shape, _mybir.dt.from_np(a.dtype), kind="ExternalInput").ap()
    for name in ("sBre", "sBim"):
        A[name] = A[name].rearrange("p (a b) -> p a b", a=8)
    for name in ("sCre", "sCim"):
        A[name] = A[name].rearrange("p (a b) -> p a b", a=32)
    A["mbias"] = A["mbias"].rearrange("p (a b) -> p a b", a=4)
    A["rscratch"] = nc.dram_tensor("rscratch", (16, 512), F32, kind="Internal").ap()
    out = nc.dram_tensor("out_0", (D, T), F32, kind="ExternalOutput").ap()
    program(nc, A, out, STAGE)
    r = _run(nc, [arrays], core_ids=[0])
    got = r.results[0]["out_0"]
    return _np.ascontiguousarray(got.T).reshape(1, T, D)
```

```python
from contextlib import ExitStack
import math

import numpy as np
import concourse.bass as bass
from concourse import mybir

F32 = mybir.dt.float32
U32 = mybir.dt.uint32
I32 = mybir.dt.int32
F32R = mybir.dt.float32r
ALU = mybir.AluOpType
ACT = mybir.ActivationFunctionType
AX = mybir.AxisListType

T = 256
D = 1024
NSLOT = 6
SCR = 23500
UNIT = 3072
NEXP = 32
CAP = 64
FF_TILES = 22
NEG = -1e30
MAGIC = 12582912.0
TWO_PI = 2.0 * math.pi

SMALL = [
    ("attn_g", 8), ("mem_g", 8), ("ffn_g", 8), ("b_gk", 2), ("gla_g", 1), ("mbq_g", 1), ("mbk_g", 1),
    ("mq_g", 1), ("mk_g", 1), ("norm_g", 128), ("subln_g", 1), ("lam_re", 32), ("lam_im", 32),
    ("log_dt", 32), ("ssm_d", 8), ("b_glu", 16), ("lamv", 256), ("rbias", 36), ("w_r", 288),
    ("w_gk", 256), ("relb", 16),
]
CONST = [
    ("ident", 128), ("anti", 128), ("onesD", 128), ("onesB", 128), ("ones128", 128), ("mask", 128), ("tiew", 8),
    ("eps", 1), ("zero", 1), ("halfpi", 1), ("scanm", 256), ("tvec", 256), ("bucket", 512), ("cut", 512),
    ("before", 128), ("ones", 128),
]


def columns(table):
    at, out = 0, {}
    for name, n in table:
        out[name] = (at, at + n)
        at += n
    return out, at


SCOL, NSC = columns(SMALL)
CCOL, NCC = columns(CONST)


class Eng:

    def __init__(self, name, sem):
        self.name, self.sem, self.n, self.q, self.seen = name, sem, 0, [], {}

    def wait(self, *toks):
        for t in toks:
            if t is None:
                continue
            sem, v = t
            if self.seen.get(id(sem), 0) >= v:
                continue
            self.seen[id(sem)] = v
            self.q.append(lambda e, sem=sem, v=v: e.wait_ge(sem, v))

    def do(self, fn, *toks, inc=True):
        self.wait(*toks)
        if inc:
            self.n += 1
            self.q.append(lambda e, sem=self.sem: fn(e).then_inc(sem, 1))
            return (self.sem, self.n)
        self.q.append(fn)
        return None

    def enter(self, sem):
        self.saved = (self.sem, self.n, self.q, self.seen)
        self.sem, self.n, self.q, self.seen = sem, 0, [], {}

    def leave(self, flag):
        part = self.q
        self.sem, self.n, self.q, self.seen = self.saved

        def body(e):
            v = e.value_load(flag)
            with e.If(v != 0):
                for f in part:
                    f(e)
        self.q.append(body)

    @property
    def last(self):
        return (self.sem, self.n) if self.n else None


def program(nc, A, out):
    with ExitStack() as ctx, ExitStack() as ctx_areas:
        def sb(name, shape, dt=F32):
            return ctx.enter_context(nc.sbuf_tensor(name, shape, dt))

        def sem(name):
            return ctx.enter_context(nc.semaphore(name))

        pe, act, dve, pool = (Eng(n, sem("s_" + n)) for n in ("pe", "act", "dve", "pool"))
        ring = sb("ring", [128, NSLOT, UNIT])
        s_ring = [sem(f"s_ring{i}") for i in range(NSLOT)]
        xT = sb("xT", [128, 8, T])
        hT = sb("hT", [128, 8, T])
        sq = sb("sq", [128, 8, T])
        small = sb("small", [128, NSC])
        cst = sb("cst", [128, NCC])
        rstd = sb("rstd", [128, 2, 2 * T])
        flag = sb("flag", [1, 1], I32)
        area = {"n": 0}

        def part(kind):
            if "ctx" in area:
                area["ctx"].close()
            c = area["ctx"] = ctx_areas.enter_context(ExitStack())
            area["n"] += 1
            n = area["n"]
            get = lambda name, shape, dt: c.enter_context(nc.sbuf_tensor(f"{name}{n}", shape, dt))
            if kind == "scr":
                area["scr"] = get("scr", [128, SCR], F32)
            elif kind == "moe":
                area["scr"] = get("scr", [128, SCR - 17408], F32)
                for name, shape in (("ws", [128, 6, 2, 1024]), ("xp", [128, 2, 2, 8, 128]), ("mh", [128, 4, 2, 128])):
                    area[name] = get(name, shape, F32R)
            else:
                for name, shape in (("gu", [128, 2, 2, 2048]), ("dn", [128, 3, 2, 1024]), ("hx", [128, 2, 8, T]),
                                    ("hh", [128, 2, 2, T])):
                    area[name] = get(name, shape, F32R)
        acc = ctx.enter_context(nc.psum_tensor("acc", [128, 4, 512], F32))
        wkt = [ctx.enter_context(nc.psum_tensor(f"wk{i}", [128, 512], F32)) for i in range(4)]

        def sm(name, a=0, b=None):
            s, e = SCOL[name]
            return small[:, s + a:(e if b is None else s + b)]

        def cs(name, a=0, b=None):
            s, e = CCOL[name]
            return cst[:, s + a:(e if b is None else s + b)]

        units = []
        released = {}
        branch = {}
        s_ringb = [sem(f"s_ringb{i}") for i in range(NSLOT)]

        def unit(src, ncols):
            n = len(units)
            units.append((src, ncols))
            if branch.get("on"):
                s = (n + branch["at"]) % NSLOT
                return n, ring[:, s, 0:ncols], (s_ringb[s], 16 * (n // NSLOT + 1))
            s = n % NSLOT
            return n, ring[:, s, 0:ncols], (s_ring[s], 16 * (n // NSLOT + 1))

        def release(n, tok):
            released[n] = tok

        def chunk(src):
            n, w, t = unit(src, 2048)
            return n, w.rearrange("p (k n) -> p k n", k=8), t

        loads = []

        def load(dst, src, *toks):
            s = sem(f"s_ld{len(loads)}")
            loads.append(s)
            act.wait(*toks)
            act.q.append(lambda e: e.dma_start(dst, src).then_inc(s, 16))
            return (s, 16)

        wk_free = [None] * 4
        wk_at = [0]
        wk_n = [4]

        def bank():
            i = wk_at[0] % wk_n[0]
            wk_at[0] += 1
            free = wk_free[i]
            assert free != "busy"
            wk_free[i] = "busy"
            return i, wkt[i], free

        acc_free = [None]

        def mm(out_, lhsT, rhs, start, stop, *toks, inc=False, skip=False):
            return pe.do(lambda e: e.matmul(out_, lhsT, rhs, start=start, stop=stop, skip_group_check=skip),
                         *toks, inc=inc)

        def tr(out_, in_, *toks, inc=False):
            return pe.do(lambda e: e.transpose(out_, in_, cs("ident")), *toks, inc=inc)

        def A_(out_, in_, func, *toks, **kw):
            return act.do(lambda e: e.activation(out_, in_, func, **kw), *toks, act.last)

        def tt(out_, a, b, op, *toks, eng=None):
            g = eng or dve
            return g.do(lambda e: e.tensor_tensor(out_, a, b, op), *toks, g.last)

        def ts(out_, a, s1, s2, op0, op1, *toks, eng=None):
            g = eng or dve
            if s2 is None:
                return g.do(lambda e: e.tensor_scalar(out_, a, s1, None, op0), *toks, g.last)
            return g.do(lambda e: e.tensor_scalar(out_, a, s1, s2, op0, op1), *toks, g.last)

        def stt(out_, a, s, b, op0, op1, *toks):
            return dve.do(lambda e: e.scalar_tensor_tensor(out=out_, in0=a, scalar=s, in1=b, op0=op0, op1=op1),
                          *toks, dve.last)

        def cp(out_, a, *toks):
            return dve.do(lambda e: e.tensor_copy(out_, a), *toks, dve.last)

        def memset(out_, v, *toks, eng=None):
            g = eng or dve
            return g.do(lambda e: e.memset(out_, v), *toks, g.last)

        def recip(out_, a, *toks):
            return dve.do(lambda e: e.reciprocal(out_, a), *toks, dve.last)

        def red(out_, a, op, *toks, negate=False, axis=AX.X):
            return dve.do(lambda e: e.tensor_reduce(out_, a, axis, op, negate=negate), *toks, dve.last)

        def fence(kind=None):
            if kind:
                part(kind)
            last = [g.last for g in (pe, act, dve, pool)]
            for g in (pe, act, dve, pool):
                g.wait(*last)

        MUL, ADD, SUB, MAX, MIN = ALU.mult, ALU.add, ALU.subtract, ALU.max, ALU.min

        t_x = load(xT[:, :, :], A["xT"].rearrange("(k p) t -> p k t", p=128))
        t_cst = load(cst[:, :], A["cst"])
        t_sm = load(small[:, :], A["small"])
        for g in (pe, act, dve, pool):
            g.wait(t_cst, t_sm)
        dve.wait(t_x)

        def bc(ap, n):
            return ap.rearrange("p (o t) -> p o t", o=1).broadcast_to([128, n, ap.shape[-1]])

        rs_free = [None, None]
        rs_at = [0]

        def stat(src, ones, ntile, groups, *toks):
            r = rs_at[0] % 2
            rs_at[0] += 1
            t = A_(sq[:, 0:ntile, :], src, ACT.Square, *toks, pe.last)
            i, b, free = bank()
            n = len(groups)
            for gi, grp in enumerate(groups):
                for k in grp:
                    tok = mm(b[:, gi * T:(gi + 1) * T], ones, sq[:, k, :], k == grp[0], k == grp[-1],
                             t, free, inc=True if k == grp[-1] else False)
            t = A_(rstd[:, r, 0:n * T], b[:, 0:n * T], ACT.Sqrt, tok, rs_free[r], bias=cs("eps"))
            wk_free[i] = t
            t = recip(rstd[:, r, 0:n * T], rstd[:, r, 0:n * T], t)
            return [rstd[:, r, g * T:(g + 1) * T] for g in range(n)], t, r

        def norm_in(dst, src, g, *toks):
            rs, t, r = stat(src[:, :, :], cs("onesD"), 8, [list(range(8))], dve.last, *toks)
            for k in range(8):
                t2 = stt(dst[:, k, :], src[:, k, :], g[:, k:k + 1], rs[0], MUL, MUL, t, pe.last)
            rs_free[r] = t2
            return t2

        def norm_add(src, g, *toks, half=False):
            i, b, free = bank()
            if half:
                ts(g, g, 0.5, None, MUL, None)
            for k in range(8):
                t = A_(sq[:, k, :], src[:, k, :], ACT.Square, *toks, pe.last)
                tok = mm(b[:, 0:T], cs("onesD"), sq[:, k, :], k == 0, k == 7, t, free, inc=(k == 7))
            r = rs_at[0] % 2
            rs_at[0] += 1
            t = A_(rstd[:, r, 0:T], b[:, 0:T], ACT.Sqrt, tok, rs_free[r], bias=cs("eps"))
            wk_free[i] = t
            t = recip(rstd[:, r, 0:T], rstd[:, r, 0:T], t)
            out_ = []
            for k in range(8):
                stt(sq[:, k, :], src[:, k, :], g[:, k:k + 1], rstd[:, r, 0:T], MUL, MUL, tok)
                out_.append(tt(xT[:, k, :], xT[:, k, :], sq[:, k, :], ADD))
            acc_free[0] = dve.last
            rs_free[r] = dve.last
            return out_

        def acc_tile(k):
            return acc[:, k // 2, (k % 2) * T:(k % 2 + 1) * T]

        acc3 = acc[:, :, :].rearrange("p b (h t) -> p (b h) t", t=T)

        def lin_fm(lhs, nk, rhs, ntiles, evac, *toks):
            for i0 in range(0, ntiles, 2):
                n = min(2, ntiles - i0)
                i, b, free = bank()
                for j in range(n):
                    for k in range(nk):
                        tok = mm(b[:, j * T:(j + 1) * T], lhs(k, i0 + j), rhs(k), k == 0, k == nk - 1,
                                 *toks, free, inc=(k == nk - 1 and j == n - 1))
                wk_free[i] = evac(i0, n, b, tok)

        def lin_acc(nk, lhs, rhs, *toks, k0=True, k1=True, tiles=range(8)):
            for k in range(nk):
                for d in tiles:
                    tok = mm(acc_tile(d), lhs(k, d), rhs(k), k0 and k == 0 and d % 2 == 0,
                             k1 and k == nk - 1, *toks, acc_free[0], inc=(k == nk - 1 and d == tiles[-1]), skip=True)
            return tok

        gb_free = {"s": [None] * 3, "h": [None] * 3}

        def glu(src, nunits, rhs, gsil, ghid, scale=None, *toks):
            pend = []
            state = {"last": None}

            def down(f, h, th, un, w, last):
                for d in range(8):
                    off = 2048 + d * 128
                    tok = mm(acc_tile(d), w[:, off:off + 128], h, f == 0 and d % 2 == 0, last,
                             th, acc_free[0], inc=(d == 7), skip=True)
                gb_free["h"][f % 3] = tok
                release(un, tok)
                state["last"] = tok

            for f in range(nunits):
                un, w, tw = unit(src[f], UNIT)
                w3 = w[:, 0:2048].rearrange("p (k a n) -> p a k n", a=2, k=8)
                i, b, free = bank()
                for a in range(2):
                    for k in range(8):
                        tok = mm(b[:, a * T:(a + 1) * T], w3[:, a, k, :], rhs(k), k == 0, k == 7,
                                 tw, free, *toks, inc=(a == 1 and k == 7))
                s, h = gsil[:, f % 3, :], ghid[:, f % 3, :]
                t1 = A_(s, b[:, 0:T], ACT.Silu, tok, gb_free["s"][f % 3])
                t2 = tt(h, s, b[:, T:2 * T], MUL, t1, gb_free["h"][f % 3])
                wk_free[i] = t2
                gb_free["s"][f % 3] = t2
                if scale is not None:
                    row, tr_ = scale(f)
                    t2 = tt(h, h, row, MUL, tr_)
                pend.append((f, h, t2, un, w, f == nunits - 1))
                if len(pend) > 1:
                    down(*pend.pop(0))
            down(*pend.pop(0))
            return state["last"]

        def project(src, x, *toks):
            for c in range(4):
                un, wo, tw = chunk(src[c])
                tok = lin_acc(8, lambda k, d: wo[:, k, (d % 2) * 128:(d % 2 + 1) * 128], lambda k: x[:, k, :],
                              tw, *toks, tiles=range(2 * c, 2 * c + 2))
                release(un, tok)
            return tok

        class Scr:
            def __init__(self):
                self.at = 0

            def get(self, *shape):
                n = int(np.prod(shape))
                ap = area["scr"][:, self.at:self.at + n]
                self.at += n
                assert self.at <= SCR, self.at
                if len(shape) == 2:
                    ap = ap.rearrange("p (a b) -> p a b", a=shape[0])
                elif len(shape) == 3:
                    ap = ap.rearrange("p (a b c) -> p a b c", a=shape[0], b=shape[1])
                return ap

        def softmax_rows(S, st, *toks, src=None):
            src = S if src is None else src
            t = red(st[:, 0, :], src, MAX, *toks, negate=True)
            for q in range(2):
                t = A_(S[:, q, :], src[:, q, :], ACT.Exp, t, bias=st[:, 0, q:q + 1], accum_out=st[:, 1, q:q + 1])
            return recip(st[:, 2, :], st[:, 1, :], t)

        def transpose_p(P, pT, *toks, free_pT=None):
            i, b, free = bank()
            for kt in range(2):
                for q in range(2):
                    t = tr(b[:, kt * T + q * 128:kt * T + (q + 1) * 128], P[:, q, kt * 128:(kt + 1) * 128],
                           *toks, free, inc=(kt == 1 and q == 1))
            t2 = A_(pT, b[:, :].rearrange("p (a b) -> p a b", a=2), ACT.Copy, t, free_pT)
            wk_free[i] = t2
            return t, t2

        part("scr")
        S1 = Scr()
        mix = S1.get(8, T)
        vtm = S1.get(2, 768)
        mh = S1.get(8, T)
        base_at = S1.at
        qz = S1.get(4, T)
        kinv = S1.get(2, T)
        kendT = S1.get(2, T)
        kend = S1.get(2, 2, 128)
        rsil = S1.get(4, T)
        ATm = S1.get(4, 2, 128)
        Sst = S1.get(3, 2 * T)
        cum = S1.get(2, T)
        gl = S1.get(2, T)
        expP = S1.get(2, T)
        expN = S1.get(2, T)
        expE = S1.get(2, T)
        lrT = S1.get(T)
        S1b = Scr()
        S1b.at = base_at
        mqz = S1b.get(4, T)
        mk = S1b.get(2, T)
        vz = S1b.get(2, 4, 128)
        Sb = [S1b.get(2, T) for _ in range(3)]
        pT = [S1b.get(2, T) for _ in range(2)]
        st = [S1b.get(3, 2) for _ in range(3)]
        mbias = S1b.get(4, 2 * T)

        memx = hT
        t_mem = load(memx[:, :, :], A["memT"].rearrange("(k p) t -> p k t", p=128))

        z0 = memset(qz, 0.0)
        z1 = memset(ATm, 0.0)
        t_mh = norm_in(mh, memx, sm("mem_g"), t_mem)
        t_h = norm_in(hT, xT, sm("attn_g"), t_x)

        un, w, tw = unit(A["u_q"], 8 * 272)
        w0 = w.rearrange("p (k n) -> p k n", k=8)
        i, b, free = bank()
        for k in range(8):
            tok = mm(b[0:16, 0:T], w0[:, k, 256:272], hT[:, k, :], k == 0, k == 7, tw, t_h, free, inc=(k == 7))
        t_lr = A_(lrT[0:16, :], b[0:16, 0:T], ACT.Copy, tok)
        wk_free[i] = t_lr
        i, b, free = bank()
        for j in range(2):
            tok = mm(b[:, j * T:(j + 1) * T], sm("w_gk")[0:16, j * 128:(j + 1) * 128], lrT[0:16, :], True, True,
                     t_lr, free, inc=(j == 1))
        for j in range(2):
            bj = b[:, j * T:(j + 1) * T]
            t = ts(cum[:, j, :], bj, sm("b_gk", j, j + 1), 0.0, ADD, MIN, tok)
        for j in range(2):
            t2 = A_(gl[:, j, :], b[:, j * T:(j + 1) * T], ACT.Abs, t, bias=sm("b_gk", j, j + 1))
        wk_free[i] = t2
        t2 = A_(gl, gl, ACT.Exp, scale=-1.0)
        t2 = A_(gl, gl, ACT.Ln, bias=1.0)
        t = tt(gl, cum, gl, SUB, t2)
        for j in range(2):
            t = dve.do(lambda e, j=j: e.tensor_tensor_scan(cum[:, j, :], cs("scanm"), gl[:, j, :], 0.0, MUL, ADD),
                       dve.last)
        A_(expP, cum, ACT.Exp, t, scale=1.0 / 16)
        t_n = A_(expN, cum, ACT.Exp, t, scale=-1.0 / 16)
        cl = cum.rearrange("p a (c t) -> p (a c) t", t=64)
        t = tt(gl.rearrange("p a (c t) -> p (a c) t", t=64), cl, cl[:, :, 63:64].broadcast_to([128, 8, 64]), SUB)
        t_e = A_(expE, gl, ACT.Exp, t, scale=-1.0 / 16)

        def q_evac(i0, n, b, tok):
            for j in range(2):
                for o in range(2):
                    p = slice(64 * o, 64 * o + 64)
                    t = stt(qz[p, 2 * j + o, :], b[p, j * T:(j + 1) * T], 0.125, expP[p, j, :], MUL, MUL, tok, t_n, z0)
            return t

        def k_evac(i0, n, b, tok):
            b3 = b[:, :].rearrange("p (a t) -> p a t", a=2)
            tt(kinv, b3, expN, MUL, tok, t_n)
            return tt(kendT, b3, expE, MUL, t_e)

        lin_fm(lambda k, i: w0[:, k, i * 128:(i + 1) * 128], 8, lambda k: hT[:, k, :], 2, q_evac, tw)
        t_q = dve.last
        release(un, pe.last)
        un, w0, tw = chunk(A["u_in"][0])
        lin_fm(lambda k, i: w0[:, k, i * 128:(i + 1) * 128], 8, lambda k: hT[:, k, :], 2, k_evac, tw)
        t_k = dve.last
        release(un, pe.last)

        for c in range(3):
            un, w1, tw = chunk(A["u_in"][1 + c])
            for q in range(2):
                i, b, free = bank()
                for k in range(8):
                    tok = mm(b[:, 0:256], hT[:, k, q * 128:(q + 1) * 128], w1[:, k, :], k == 0, k == 7,
                             tw, free, inc=(k == 7))
                wk_free[i] = A_(vtm[:, q, c * 256:(c + 1) * 256], b[:, 0:256], ACT.Copy, tok)
            release(un, tok)
        t_v = act.last

        for bb in range(2):
            i, b, free = bank()
            for h in range(4):
                tok = mm(b[:, h * 128:(h + 1) * 128], kinv[:, h // 2, bb * 128:(bb + 1) * 128],
                         qz[:, h, bb * 128:(bb + 1) * 128], True, True, t_q, t_k, free, inc=(h == 3))
            mk_ = cs("mask").bitcast(U32).rearrange("p (o t) -> p o t", o=1).broadcast_to([128, 4, 128])
            t = dve.do(lambda e, b=b, bb=bb, mk_=mk_: e.copy_predicated(
                ATm[:, :, bb, :], mk_, b[:, :].rearrange("p (h t) -> p h t", h=4)), tok, z1, dve.last)
            wk_free[i] = t
        t_A = dve.last
        i, b, free = bank()
        for bb in range(2):
            for p in range(2):
                tok = tr(b[:, (bb * 2 + p) * 128:(bb * 2 + p + 1) * 128], kendT[:, p, bb * 128:(bb + 1) * 128], t_k, free,
                         inc=(bb == 1 and p == 1))
        t_ke = A_(kend, b[:, :].rearrange("p (a b c) -> p a b c", a=2, b=2), ACT.Copy, tok)
        wk_free[i] = t_ke
        dS = []
        for n in range(3):
            i, b, free = bank()
            r = slice(64 * (n % 2), 64 * (n % 2) + 64)
            for p in range(2):
                tok = mm(b[:, p * T:(p + 1) * T], kend[r, n // 2, p, :], vtm[r, n // 2, p * T:(p + 1) * T], True, True,
                         t_ke, t_v, free, inc=(p == 1))
            if n == 0:
                t = cp(Sst[:, 0, :], b[:, :], tok)
            else:
                for p in range(2):
                    t = stt(Sst[:, n, p * T:(p + 1) * T], Sst[:, n - 1, p * T:(p + 1) * T],
                            expP[:, p, 64 * n + 63:64 * n + 64], b[:, p * T:(p + 1) * T], MUL, ADD, tok)
            wk_free[i] = t
        t_S = dve.last
        for h in range(4):
            p = h // 2
            o = acc[:, p, (h % 2) * T:(h % 2 + 1) * T]
            for bb in range(2):
                mm(o[:, bb * 128:(bb + 1) * 128], vtm[:, bb, h * 128:(h + 1) * 128], ATm[:, h, bb, :],
                   h % 2 == 0 and bb == 0, False, t_A, t_v, skip=True)
            for n in range(1, 4):
                tok = mm(o[:, n * 64:(n + 1) * 64], Sst[:, n - 1, p * T + (h % 2) * 128:p * T + (h % 2 + 1) * 128],
                         qz[:, h, n * 64:(n + 1) * 64], False, True, t_S, inc=(n == 3), skip=True)
        t_o = tok

        for c in range(2):
            un, w2, tw = chunk(A["u_in"][4 + c])

            def r_evac(i0, n, b, tok):
                return A_(rsil[:, 2 * c:2 * c + 2, :], b[:, :].rearrange("p (a t) -> p a t", a=2), ACT.Silu, tok)

            lin_fm(lambda k, i: w2[:, k, i * 128:(i + 1) * 128], 8, lambda k: hT[:, k, :], 2, r_evac, tw)
            release(un, pe.last)
        t_r = act.last

        o3 = acc3[:, 0:4, :]
        for p in range(2):
            rs, t, r = stat(o3[:, 2 * p:2 * p + 2, :], cs("ones128"), 2, [[0], [1]], t_o)
            for j in range(2):
                h = 2 * p + j
                stt(mix[:, h, :], o3[:, h, :], sm("gla_g"), rs[j], MUL, MUL, t)
                t2 = tt(mix[:, h, :], mix[:, h, :], rsil[:, h, :], MUL, t_r)
            rs_free[r] = t2
        acc_free[0] = dve.last
        t_gla = dve.last
        fence()

        t_mb = load(mbias, A["mbias"], dve.last, act.last, pe.last)
        z0 = memset(mqz, 0.0)
        z2 = memset(vz, 0.0)

        def normed(src, gname, dst_z, dst_f, rhs, z=None):
            un, wv, tw = chunk(src)

            def ev(i0, n, b, tok):
                b3 = b[:, :].rearrange("p (a t) -> p a t", a=2)
                rs, t, r = stat(b3, cs("onesB"), 2, [[0], [1]], tok)
                for j in range(2):
                    if dst_f is not None:
                        t2 = stt(dst_f[:, j, :], b3[:, j, :], sm(gname), rs[j], MUL, MUL, t)
                    else:
                        for o in range(2):
                            p = slice(64 * o, 64 * o + 64)
                            t2 = stt(dst_z[p, 2 * j + o, :], b3[p, j, :], sm(gname)[p, :], rs[j][p, :], MUL, MUL, t, z)
                rs_free[r] = t2
                return t2
            lin_fm(lambda k, i: wv[:, k, i * 128:(i + 1) * 128], 8, rhs, 2, ev, tw)
            release(un, pe.last)
            return dve.last

        def attend(qzt, kf, vzt, bias, first, t_in):
            for pr in range(2):
                bo, freeo = acc[:, pr, :], acc_free[0]
                for j in range(2):
                    h = 2 * pr + j
                    i, b, free = bank()
                    for q in range(2):
                        tok = mm(b[:, q * T:(q + 1) * T], qzt[:, h, q * 128:(q + 1) * 128], kf[:, h // 2, :], True, True,
                                 t_in, free, inc=(q == 1))
                    S, s_ = Sb[h % 3], st[h % 3]
                    b3 = b[:, :].rearrange("p (a t) -> p a t", a=2)
                    if bias is not None:
                        t = stt(S, b3, 0.125, bias[:, h, :].rearrange("p (a t) -> p a t", a=2), MUL, ADD, tok, t_mb, pe.last)
                    else:
                        t = ts(S, b3, 0.125, None, MUL, None, tok, pe.last)
                    wk_free[i] = t
                    t = softmax_rows(S, s_, t)
                    for q in range(2):
                        t = ts(S[:, q, :], S[:, q, :], s_[:, 2, q:q + 1], None, MUL, None, t)
                    _, t = transpose_p(S, pT[h % 2], t, free_pT=pe.last)
                    for kt in range(2):
                        tok = mm(bo[:, 0:T], vzt[:, kt, h, :], pT[h % 2][:, kt, :], j == 0 and kt == 0,
                                 j == 1 and kt == 1, t, freeo, inc=(kt == 1))
                last = A_(mix[:, first + pr, :], bo[:, 0:T], ACT.Copy, tok)
            acc_free[0] = last

        normed(A["u_in"][6], "mbq_g", mqz, None, lambda k: hT[:, k, :], z0)
        t_k = normed(A["u_in"][7], "mbk_g", None, mk, lambda k: hT[:, k, :])
        for h in range(4):
            o = 64 * (h % 2)
            t = cp(vz[:, :, h, o:o + 64], vtm[:, :, 512 + h * 64:512 + h * 64 + 64], t_v, z2)
        attend(mqz, mk, vz, mbias, 4, t)
        t_mz = memset(mqz, 0.0, pe.last)
        normed(A["u_in"][8], "mq_g", mqz, None, lambda k: hT[:, k, :], t_mz)
        dve.wait(pe.last)
        normed(A["u_mem"][0], "mk_g", None, mk, lambda k: mh[:, k, :])
        un, w4, tw = chunk(A["u_mem"][1])
        for q in range(2):
            i, b, free = bank()
            for k in range(8):
                tok = mm(b[:, 0:256], mh[:, k, q * 128:(q + 1) * 128], w4[:, k, :], k == 0, k == 7, tw, free, inc=(k == 7))
            for h in range(4):
                o = 64 * (h % 2)
                t = cp(vz[:, q, h, o:o + 64], b[:, h * 64:h * 64 + 64], tok)
            wk_free[i] = t
        release(un, pe.last)
        attend(mqz, mk, vz, None, 6, dve.last)
        t_mix = act.last

        tok = project(A["u_out"], mix, t_mix)
        t = tt(xT[:, :, :], xT[:, :, :], acc3, ADD, tok)
        acc_free[0] = t

        def finish(src=xT):
            s = sem("s_fin")
            act.wait(dve.last, act.last)
            act.q.append(lambda e: e.dma_start(out.rearrange("(k p) t -> p k t", p=128), src[:, :, :]).then_inc(s, 16))
            act.q.append(lambda e: e.wait_ge(s, 16))

        def emit():
            block = ctx.enter_context(nc.Block())

            @block.sync
            def _(e):
                for n, (src, ncols) in enumerate(units):
                    if n == branch.get("at"):
                        e.wait_ge(*branch["flag"])
                        v = e.value_load(flag[0:1, 0:1])
                        with e.If(v != 0):
                            for m in range(n - NSLOT, n):
                                e.wait_ge(*released[m])
                            for m, (src_b, nc_b) in enumerate(branch["units"]):
                                s = (m + n) % NSLOT
                                if m >= NSLOT:
                                    e.wait_ge(*branch["released"][m - NSLOT])
                                e.dma_start(ring[:, s, 0:nc_b], src_b).then_inc(s_ringb[s], 16)
                            for t in branch["end"]:
                                e.wait_ge(*t)
                    if n >= NSLOT:
                        e.wait_ge(*released[n - NSLOT])
                    e.dma_start(ring[:, n % NSLOT, 0:ncols], src).then_inc(s_ring[n % NSLOT], 16)

            def play(g):
                def body(e):
                    for f in g.q:
                        f(e)
                return body

            block.tensor(play(pe))
            block.vector(play(dve))
            block.scalar(play(act))
            block.gpsimd(play(pool))

        fence("moe")
        S2 = Scr()
        WS, Xp, MH = area["ws"], area["xp"], area["mh"]
        L = S2.get(2, 36)
        R = S2.get(2, 96)
        comb = S2.get(2, 32)
        combT = S2.get(T)
        t_h = norm_in(hT, xT, sm("ffn_g"))
        wr = sm("w_r").rearrange("p (k n) -> p k n", k=8)
        i, b, free = bank()
        for q in range(2):
            for k in range(8):
                tok = mm(b[:, q * 36:(q + 1) * 36], hT[:, k, q * 128:(q + 1) * 128], wr[:, k, :], k == 0, k == 7, t_h,
                         free, inc=(k == 7 and q == 1))
        rb = sm("rbias").rearrange("p (o t) -> p o t", o=1).broadcast_to([128, 2, 36])
        t = tt(L, b[:, 0:72].rearrange("p (a n) -> p a n", a=2), rb, ADD, tok)
        wk_free[i] = t

        def onehot(dst, src, mx, n):
            tt(dst, src, mx.broadcast_to([128, 2, n]), ALU.is_ge)
            tw_ = cs("tiew").rearrange("p (o t) -> p o t", o=1)[:, :, 0:n].broadcast_to([128, 2, n])
            tt(dst, dst, tw_, MUL)
            m = R[:, :, 95:96]
            red(m, dst, MAX)
            return tt(dst, dst, m.broadcast_to([128, 2, n]), ALU.is_equal)

        gm, goh, gex, gsum = R[:, :, 0:1], R[:, :, 1:5], R[:, :, 5:9], R[:, :, 9:10]
        les, m1, oh1, les2, m2, oh2 = R[:, :, 10:18], R[:, :, 18:19], R[:, :, 19:27], R[:, :, 27:35], R[:, :, 35:36], R[:, :, 36:44]
        e2, p1, p2, c8 = R[:, :, 44:45], R[:, :, 45:46], R[:, :, 46:47], R[:, :, 48:56]
        red(gm, L[:, :, 0:4], MAX)
        onehot(goh, L[:, :, 0:4], gm, 4)
        t = tt(gex, L[:, :, 0:4], gm.broadcast_to([128, 2, 4]), SUB)
        t = A_(gex, gex, ACT.Exp, t)
        red(gsum, gex, ADD, t)
        for g in range(4):
            src = L[:, :, 4 + 8 * g:12 + 8 * g]
            oh = goh[:, :, g:g + 1].broadcast_to([128, 2, 8])
            if g == 0:
                tt(les, src, oh, MUL)
            else:
                tt(les2, src, oh, MUL)
                tt(les, les, les2, ADD)
        red(m1, les, MAX)
        onehot(oh1, les, m1, 8)
        ts(les2, oh1, -3e38, None, MUL, None)
        tt(les2, les2, les, ADD)
        red(m2, les2, MAX)
        onehot(oh2, les2, m2, 8)
        t = tt(e2, m2, m1, SUB)
        t = A_(e2, e2, ACT.Exp, t)
        ts(p1, e2, 1.0, None, ADD, None, t)
        tt(p1, p1, gsum, MUL)
        recip(p1, p1)
        tt(p2, p1, e2, MUL)
        tt(R[:, :, 64:72], oh1, oh2, ADD)
        tt(oh1, oh1, p1.broadcast_to([128, 2, 8]), MUL)
        tt(oh2, oh2, p2.broadcast_to([128, 2, 8]), MUL)
        tt(c8, oh1, oh2, ADD)
        for g in range(4):
            t = tt(comb[:, :, 8 * g:8 * g + 8], c8, goh[:, :, g:g + 1].broadcast_to([128, 2, 8]), MUL)

        h2 = S2.get(2, 1024)
        M = S2.get(2, 32)
        posm = S2.get(2, 32)
        late = S2.get(2, 32)
        mx = S2.get(2)
        Sel = [S2.get(2, 2, 64) for _ in range(2)]
        SG = [S2.get(2, 128) for _ in range(2)]
        G = [S2.get(T) for _ in range(2)]
        ysm = [sq[:, 4 * x:4 * x + 4, :].rearrange("p a t -> p (a t)") for x in range(2)]
        msil = [S2.get(128) for _ in range(3)]
        for g in range(4):
            ohg = goh[:, :, g:g + 1].broadcast_to([128, 2, 8])
            t = tt(M[:, :, 8 * g:8 * g + 8], R[:, :, 64:72], ohg, MUL)
        i, b, free = bank()
        mm(b[:, 0:32], cs("before"), M[:, 0, :], True, True, t, free)
        mm(b[:, 32:64], cs("ones"), M[:, 0, :], True, False)
        mm(b[:, 32:64], cs("before"), M[:, 1, :], False, True)
        mm(b[:, 64:96], cs("ones"), M[:, 0, :], True, False)
        tok = mm(b[:, 64:96], cs("ones"), M[:, 1, :], False, True, inc=True)
        rank = b[:, 0:64].rearrange("p (a n) -> p a n", a=2)
        ts(late, rank, float(CAP), None, ALU.is_ge, None, tok)
        tt(late, late, comb, MUL)
        red(mx[:, 0:1], b[:, 64:96], MAX)
        t_fl = ts(flag[:, :], mx[0:1, 0:1], float(CAP), None, ALU.is_gt, None)
        ts(posm, rank, 1.0, None, ADD, None)
        wk_free[i] = dve.last
        tt(posm, posm, M, MUL)
        t_pos = ts(posm, posm, -1.0, None, ADD, None)
        for q in range(2):
            for hf in range(2):
                i, b, free = bank()
                for k in range(4):
                    tok = tr(b[:, k * 128:(k + 1) * 128], hT[:, 4 * hf + k, q * 128:(q + 1) * 128], free, inc=(k == 3))
                wk_free[i] = A_(h2[:, q, hf * 512:(hf + 1) * 512], b[:, :], ACT.Copy, tok)
        t_h2 = act.last

        pe.wait(*wk_free)
        y_free = [None] * 4
        NP = NEXP // 2
        it64 = cs("tvec", 0, 64).rearrange("p (a b t) -> p a b t", a=1, b=1).broadcast_to([128, 2, 2, 64])
        t_sg, t_G, t_X, t_ysm, f_X, f_ysm, f_sg, f_G = {}, {}, {}, {}, {}, {}, {}, {}

        def choose(p):
            x = p % 2
            v = posm[:, :, 2 * p:2 * p + 2].rearrange("p a (b o) -> p a b o", o=1).broadcast_to([128, 2, 2, 64])
            c = comb[:, :, 2 * p:2 * p + 2].rearrange("p a (b o) -> p a b o", o=1).broadcast_to([128, 2, 2, 64])
            tt(Sel[x], v, it64, ALU.is_equal, f_sg.get(p - 2), t_pos)
            if CAP < 64:
                tt(Sel[x][:, :, :, CAP:], Sel[x][:, :, :, CAP:], Sel[x][:, :, :, CAP:], SUB)
            t_sg[p] = tt(SG[x].rearrange("p a (b t) -> p a b t", b=2), Sel[x], c, MUL)

        def gather(p, hf, i):
            x, b = p % 2, wkt[i]
            for k in range(4):
                for q in range(2):
                    kk = 4 * hf + k
                    tok = mm(b[:, k * 128:(k + 1) * 128], h2[:, q, kk * 128:(kk + 1) * 128],
                             Sel[x][:, q, :, :].rearrange("p b t -> p (b t)"), q == 0, q == 1,
                             t_sg[p], t_h2, wk_free[i], inc=(k == 3 and q == 1))
            b3 = b[:, :].rearrange("p (k t) -> p k t", k=4)
            hi, lo = (Xp[:, x, n, 4 * hf:4 * hf + 4, :] for n in range(2))
            t = A_(hi, b3, ACT.Copy, tok, f_X.get(p - 2))
            t_X[p] = wk_free[i] = tt(lo, b3, hi.bitcast(F32), SUB, t)

        def gates(p, i):
            x, b = p % 2, wkt[i]
            for q in range(2):
                tok = tr(b[:, q * 128:(q + 1) * 128], SG[x][:, q, :], t_sg[p], wk_free[i], inc=(q == 1))
            f_sg[p] = tok
            t_G[p] = wk_free[i] = cp(G[x], b[:, 0:T], tok, f_G.get(p - 2))

        def combine(p, tiles):
            x = p % 2
            for d in tiles:
                tok = mm(acc_tile(d), ysm[x][:, d * 128:(d + 1) * 128], G[x], p == 0 and d % 2 == 0, p == NP - 1,
                         *t_ysm[p], t_G[p], acc_free[0], inc=(d == tiles[-1]), skip=True)
            f_ysm[p] = f_G[p] = tok
            return tok

        s_free, h_free = [None] * 3, [None] * 4
        THREE = ((0, 0), (0, 1), (1, 0))
        wt, part_at, part_tok, ws_free = {}, {}, {}, [None] * 6
        NU = 4 * NEXP

        def split(f, a):
            if f >= NU:
                return
            if a == 0:
                wt[f] = unit(A["u_moe"][f], UNIT)
            un, w, tw = wt[f]
            n = len(part_at) % 6
            part_at[f, a] = n
            src = w[:, a * 1024:(a + 1) * 1024]
            t = A_(WS[:, n, 0, :], src, ACT.Copy, tw, ws_free[n])
            part_tok[f, a] = t = tt(WS[:, n, 1, :], src, WS[:, n, 0, :].bitcast(F32), SUB, t, ws_free[n],
                                    eng=pool if a == 2 else dve)
            if a == 2:
                release(un, t)

        def place(f):
            odd = (f // 4) % 2
            return 2 * odd + f % 2, 64 * odd

        def moe_hid(f):
            m, b = msil[f % 3], wkt[f % 2]
            o = place(f)[1]
            tok = pe.do(lambda e: e.transpose(b[:, 256:320], m[o:o + 64, :], cs("ident", o, o + 64)[o:o + 64, :]), t_m[f])
            s_free[f % 3] = tok

            def rest():
                n, o = place(f)
                hi, lo = (MH[:, n, a, o:o + 64] for a in range(2))
                t = A_(hi, b[:, 256:320], ACT.Copy, tok, h_free[n])
                t_mh[f] = wk_free[f % 2] = tt(lo, b[:, 256:320], hi.bitcast(F32), SUB, t)
            return rest

        def moe_down(f):
            p, j = f // 8, f % 8
            n_, m_ = part_at[f, 2], place(f)[0]
            for hf in range(2):
                y = wkt[2 + hf]
                for n, (x, z) in enumerate(THREE):
                    tok = mm(y[:, :], MH[:, m_, x, :], WS[:, n_, z, hf * 512:(hf + 1) * 512],
                             j == 0 and n == 0, j == 7 and n == 2, t_mh[f], part_tok[f, 2], *y_free,
                             inc=(n == 2), skip=True)
            ws_free[n_] = h_free[m_] = tok
            if j == 7:
                y_free[0] = A_(ysm[p % 2][:, 0:512], wkt[2][:, :], ACT.Copy, tok, f_ysm.get(p - 2))
                y_free[1] = cp(ysm[p % 2][:, 512:1024], wkt[3][:, :], tok, f_ysm.get(p - 2))
                t_ysm[p] = (y_free[0], y_free[1])

        A_(MH[:, :, :, :].rearrange("p a b c -> p (a b c)"), cs("zero").broadcast_to([128, 1024]), ACT.Copy)
        t_m, t_mh = {}, {}
        split(0, 0)
        split(0, 1)
        choose(0)
        gather(0, 0, 0)
        gather(0, 1, 1)
        gates(0, 0)
        split(1, 0)
        split(1, 1)
        for f in range(NU):
            e_, p, j = f // 4, f // 8, f % 8
            i = f % 2
            b, rest = wkt[i], None
            for k in range(8):
                if k == 2 and f:
                    rest = moe_hid(f - 1)
                n_ = part_at[f, k // 4]
                for n, (x, z) in enumerate(THREE):
                    tok = mm(b[:, 0:256], Xp[:, p % 2, x, k, :],
                             WS[:, n_, z, (k % 4) * 256:(k % 4 + 1) * 256], k == 0 and n == 0, k == 7 and n == 2,
                             part_tok[f, k // 4], t_X[p], wk_free[i], inc=(k % 4 == 3 and n == 2))
                if k % 4 == 3:
                    ws_free[n_] = tok
            if j == 7:
                f_X[p] = tok
            if rest:
                rest()
            split(f, 2)
            r = slice(place(f)[1], place(f)[1] + 64)
            m = msil[f % 3][r, :]
            t1 = A_(m, b[r, 0:128], ACT.Silu, tok, s_free[f % 3])
            t_m[f] = tt(m, m, b[r, 128:256], MUL, t1)
            split(f + 2, 0)
            if f:
                moe_down(f - 1)
            split(f + 2, 1)
            more = p + 1 < NP
            if j == 0 and more:
                choose(p + 1)
            if j in (2, 4) and more:
                gather(p + 1, j // 2 - 1, 1 - i)
            if j in (2, 4, 6) and p:
                combine(p - 1, {2: range(0, 3), 4: range(3, 6), 6: range(6, 8)}[j])
            if j == 6 and more:
                gates(p + 1, 1 - i)
        moe_hid(NU - 1)()
        moe_down(NU - 1)
        tok = combine(NP - 1, range(8))
        t = tt(xT[:, :, :], xT[:, :, :], acc3, ADD, tok)
        acc_free[0] = t
        pe.wait(*wk_free, *y_free)

        branch["at"] = len(units)
        branch["flag"] = t_fl
        engines = (pe, act, dve)
        kept = (list(wk_free), list(rs_free), list(acc_free), wk_at[0])
        before = [g.last for g in engines]
        for g in engines:
            g.wait(t_fl)
        for g in engines:
            g.enter(sem("s_b" + g.name))
            g.wait(*before)
        wk_free[:] = [None] * 4
        acc_free[0] = None
        gb_free["s"] = [None] * 3
        gb_free["h"] = [None] * 3
        i, b, free = bank()
        for q in range(2):
            tok = tr(b[0:32, q * 128:(q + 1) * 128], late[:, q, :], inc=(q == 1))
        t_cT = cp(combT[0:32, :], b[0:32, 0:T], tok)
        wk_free[i] = t_cT
        row = {}
        cb_free = [None, None]
        pick_free = [None, None]
        gsil, ghid = (h2[:, n, 0:3 * T].rearrange("p (a t) -> p a t", a=3) for n in range(2))
        cb = [h2[:, n, 3 * T:4 * T] for n in range(2)]

        def expert_row(f):
            e_ = f // 4
            if e_ not in row:
                i, b, free = bank()
                pick = G[e_ % 2][0:32, 0:128]
                t = cp(pick, cs("ident", e_, e_ + 1)[0:32, :].broadcast_to([32, 128]), pick_free[e_ % 2])
                tok = mm(b[:, 0:T], pick, combT[0:32, :], True, True, t_cT, t, free, inc=True)
                pick_free[e_ % 2] = tok
                t = A_(cb[e_ % 2], b[:, 0:T], ACT.Copy, tok, cb_free[e_ % 2])
                wk_free[i] = t
                row[e_] = t
            if f % 4 == 3:
                cb_free[e_ % 2] = (dve.sem, dve.n + 1)
            return cb[e_ % 2], row[e_]

        main_units, main_released = list(units), dict(released)
        del units[:]
        released.clear()
        branch["on"] = True
        tok = glu([A["u_moe"][u] for u in range(128)], 128, lambda k: hT[:, k, :], gsil, ghid, expert_row)
        tt(xT[:, :, :], xT[:, :, :], acc3, ADD, tok)
        branch["units"], branch["released"] = list(units), dict(released)
        units[:], branch["on"] = main_units, False
        released.clear()
        released.update(main_released)
        ends = [g.last for g in engines]
        for g in engines:
            g.wait(*ends)
        branch["end"] = ends
        for g in engines:
            g.leave(flag[0:1, 0:1])
        wk_free[:], rs_free[:], acc_free[:], wk_at[0] = kept

        def ffn(i, j, xtok):
            fence("ffn")
            GU, DN, HX, HH = (area[n] for n in ("gu", "dn", "hx", "hh"))
            a = (i * 8 + 4 * j) * 8
            g = sm("norm_g", a, a + 8)
            NF = FF_TILES
            t_hx, t_sq = [], []
            wt = {}
            t_gu, t_dn = {}, {}
            f_gu, f_dn = {}, {}

            def split_gu(f):
                wt[f] = un, w, tw = unit(A["u_ffn"][(2 * i + j) * FF_TILES + f], UNIT)
                hi, lo = GU[:, f % 2, 0, :], GU[:, f % 2, 1, :]
                t = A_(hi, w[:, 0:2048], ACT.Copy, tw, f_gu.get(f - 2))
                t_gu[f] = tt(lo, w[:, 0:2048], hi.bitcast(F32), SUB, t)

            def split_dn(f):
                un, w, tw = wt[f]
                hi, lo = DN[:, f % 3, 0, :], DN[:, f % 3, 1, :]
                t = A_(hi, w[:, 2048:3072], ACT.Copy, tw, f_dn.get(f - 3))
                t_dn[f] = tt(lo, w[:, 2048:3072], hi.bitcast(F32), SUB, t)
                release(un, t_dn[f])

            split_gu(0)
            split_dn(0)
            for k in range(8):
                t = A_(HX[:, 0, k, :], xT[:, k, :], ACT.Copy, xtok[k], scale=g[:, k:k + 1])
                t_hx.append(stt(HX[:, 1, k, :], xT[:, k, :], g[:, k:k + 1], HX[:, 0, k, :].bitcast(F32), MUL, SUB, t))
                t_sq.append(A_(sq[:, k, :], xT[:, k, :], ACT.Square))
            isq, bsq, freesq = bank()
            r = rs_at[0] % 2
            rs_at[0] += 1
            row = rstd[:, r, 0:T]
            THREE = ((0, 0), (0, 1), (1, 0))
            hid_free = [None, None]
            t_hid = {}

            def down(f, last):
                h, hs = HH[:, f % 2], DN[:, f % 3]
                for d in range(8):
                    for n, (x, y) in enumerate(THREE):
                        tok = mm(acc_tile(d), hs[:, x, d * 128:(d + 1) * 128], h[:, y, :],
                                 f == 0 and d % 2 == 0 and n == 0, last and n == 2,
                                 t_hid[f], t_dn[f], acc_free[0], inc=(d == 7 and n == 2), skip=True)
                hid_free[f % 2] = f_dn[f] = tok
                return tok

            for f in range(NF):
                ib, b, free = bank()
                for k in range(8):
                    if f == 0:
                        tok0 = mm(bsq[:, 0:T], cs("onesD"), sq[:, k, :], k == 0, k == 7, t_sq[k], freesq, inc=(k == 7))
                    for a_ in range(2):
                        for n, (x, y) in enumerate(THREE):
                            tok = mm(b[:, a_ * T:(a_ + 1) * T],
                                     GU[:, f % 2, x, a_ * 1024 + k * 128:a_ * 1024 + (k + 1) * 128], HX[:, y, k, :],
                                     k == 0 and a_ == 0 and n == 0, k == 7 and n == 2, t_gu[f], t_hx[k], free,
                                     inc=(k == 7 and a_ == 1 and n == 2), skip=True)
                f_gu[f] = tok
                if f == 0:
                    t = A_(row, bsq[:, 0:T], ACT.Sqrt, tok0, rs_free[r], bias=cs("eps"))
                    wk_free[isq] = t
                    recip(row, row, t)
                if f + 1 < NF:
                    split_gu(f + 1)
                G, Uu, Sg = (hT[:, 3 * (f % 2) + n, :] for n in range(3))
                t1 = tt(G, b[:, 0:T], row, MUL, tok)
                t2 = A_(Sg, G, ACT.Silu, t1)
                t3 = tt(Uu, b[:, T:2 * T], row, MUL)
                wk_free[ib] = t3
                t3 = tt(Uu, Sg, Uu, MUL, t2)
                t4 = A_(HH[:, f % 2, 0, :], Uu, ACT.Copy, t3, hid_free[f % 2])
                t_hid[f] = tt(HH[:, f % 2, 1, :], Uu, HH[:, f % 2, 0, :].bitcast(F32), SUB, t4)
                if f + 1 < NF:
                    split_dn(f + 1)
                if f:
                    down(f - 1, False)
            rs_free[r] = dve.last
            tok = down(NF - 1, True)
            return norm_add(acc3, sm("norm_g", a + 8, a + 16), tok, half=True)

        def ng(i, g):
            return sm("norm_g", (i * 8 + g) * 8, (i * 8 + g + 1) * 8)

        def ple(i):
            fence("scr")
            S = Scr()
            S.at = 1536
            pTt = S.get(2, T)
            sg = S.get(8, T)
            t_p = load(pTt, A["pT"][i].rearrange("(k p) t -> p k t", p=128), pe.last, act.last, dve.last)
            t_h = norm_in(hT, xT, ng(i, 6))
            for c4 in range(4):
                un, w, tw = unit(A["u_ple"][4 * i + c4], 2560)
                wg = w[:, 0:2048].rearrange("p (k n) -> p k n", k=8)
                wp = w[:, 2048:2560].rearrange("p (k n) -> p k n", k=2)

                def ev(i0, n, b, tok):
                    return A_(sg[:, 2 * c4:2 * c4 + 2, :], b[:, :].rearrange("p (a t) -> p a t", a=2), ACT.Sigmoid, tok)

                lin_fm(lambda k, c: wg[:, k, c * 128:(c + 1) * 128], 8, lambda k: hT[:, k, :], 2, ev, tw, t_h)
                tok = lin_acc(2, lambda k, d: wp[:, k, (d % 2) * 128:(d % 2 + 1) * 128], lambda k: pTt[:, k, :],
                              tw, t_p, tiles=range(2 * c4, 2 * c4 + 2))
                release(un, tok)
            t = tt(sg, sg, acc3, MUL, tok, act.last)
            acc_free[0] = t
            rs, t, r = stat(sg, cs("onesD"), 8, [list(range(8))], t)
            g = ng(i, 7)
            for k in range(8):
                t2 = stt(hT[:, k, :], sg[:, k, :], g[:, k:k + 1], rs[0], MUL, MUL, t, pe.last)
            rs_free[r] = t2
            return tt(xT[:, :, :], xT[:, :, :], hT[:, :, :], ADD, t2)

        xtok = ffn(0, 0, [dve.last] * 8)
        fence("scr")
        S3 = Scr()
        S3.at = 1536
        qz2 = S3.get(16, T)
        kf = S3.get(8, T)
        V = S3.get(2, 1024)
        o2 = S3.get(8, T)
        Sb2 = [S3.get(2, T) for _ in range(3)]
        aT = [S3.get(2, T) for _ in range(2)]
        bt = [S3.get(2, 384) for _ in range(2)]
        st2 = [S3.get(3, 2) for _ in range(3)]
        lam = S3.get(8)
        lm = [S3.get(2), S3.get(2)]
        rvec = S3.get(512)
        lamt = S3.get(2, 64)
        t_h = norm_in(hT, xT, ng(0, 2))
        i, b, free = bank()
        tok = mm(b[0:16, :], sm("relb")[0:32, :], cs("bucket")[0:32, :], True, True, free, inc=True)
        t = tt(rvec[0:16, :], b[0:16, :], cs("cut")[0:16, :], ADD, tok)
        wk_free[i] = t
        s_rv = sem("s_rv")
        act.wait(t)
        rdram = A["rscratch"]
        act.q.append(lambda e: e.dma_start(rdram, rvec[0:16, :]).then_inc(s_rv, 16))
        lv = sm("lamv").rearrange("p (a b n) -> p a b n", a=2, b=2)
        tt(lamt, lv[:, :, 0, :], lv[:, :, 1, :], MUL)
        t = red(lam[:, 0:2], lamt, ADD)
        t = A_(lam[:, 2:4], lam[:, 0:2], ACT.Exp, t)
        tt(lam[:, 4:5], lam[:, 2:3], lam[:, 3:4], SUB, t)
        ts(lam[:, 4:5], lam[:, 4:5], 0.8 - 0.6 * math.exp(0.0), None, ADD, None)
        z = memset(qz2, 0.0)
        tiles = []
        for u in range(8):
            un, wq, tw = chunk(A["u_qkv"][u])
            base = 2 * u

            def ev(i0, n, b, tok):
                c = base + i0
                b3 = b[:, :].rearrange("p (a t) -> p a t", a=2)
                if c >= 8:
                    return A_(kf[:, c - 8:c - 6, :], b3, ACT.Copy, tok)
                q4 = qz2[:, 2 * c:2 * c + 4, :].rearrange("p (a m) t -> p a m t", m=2)
                A_(q4[0:64, :, 0, :], b3[0:64, :, :], ACT.Copy, tok, z, scale=0.125)
                return A_(q4[64:128, :, 1, :], b3[64:128, :, :], ACT.Copy, tok, scale=0.125)

            lin_fm(lambda k, c: wq[:, k, c * 128:(c + 1) * 128], 8, lambda k: hT[:, k, :], 2, ev, tw, t_h)
            release(un, pe.last)
        for c in range(4):
            un, wv, tw = chunk(A["u_qkv"][8 + c])
            for q in range(2):
                i, b, free = bank()
                for k in range(8):
                    tok = mm(b[:, 0:256], hT[:, k, q * 128:(q + 1) * 128], wv[:, k, :], k == 0, k == 7, tw, free, inc=(k == 7))
                wk_free[i] = cp(V[:, q, c * 256:(c + 1) * 256], b[:, 0:256], tok)
            release(un, tok)
        t_qkv = [act.last, dve.last]
        bt_free = [None, None]
        aT_free = [None, None]
        for h in range(8):
            bh = bt[h % 2]
            act.wait(bt_free[h % 2], (s_rv, 16))
            sbt = []
            for m in range(2):
                src = bass.AP(tensor=rdram.tensor, offset=rdram.offset + (2 * h + m) * 512,
                              ap=[[1, 128], [1, 384]])
                sbt.append(load(bh[:, m, :], src))
            Ss = []
            for m in range(2):
                c = 2 * h + m
                i, b, free = bank()
                for q in range(2):
                    mm(b[:, q * T:(q + 1) * T], qz2[:, c, q * 128:(q + 1) * 128], kf[:, h, :], True, False,
                       *t_qkv, free)
                    tok = mm(b[:, q * T:(q + 1) * T], cs("anti"), bh[:, m, 128 - 128 * q:384 - 128 * q], False, True,
                             sbt[m], inc=(q == 1))
                bt_free[h % 2] = tok
                S, s_ = Sb2[c % 3], st2[c % 3]
                t = softmax_rows(S, s_, tok, src=b[:, :].rearrange("p (a t) -> p a t", a=2))
                wk_free[i] = act.last
                Ss.append((S, s_))
            (P0, r0), (P1, r1) = Ss
            lmh = lm[h % 2]
            t = ts(lmh, r1[:, 2, :], lam[:, 4:5], None, MUL, None, t)
            for q in range(2):
                ts(P1[:, q, :], P1[:, q, :], lmh[:, q:q + 1], None, MUL, None)
                t = stt(P0[:, q, :], P0[:, q, :], r0[:, 2, q:q + 1], P1[:, q, :], MUL, SUB)
            _, t = transpose_p(P0, aT[h % 2], t, free_pT=aT_free[h % 2])
            i, b, free = bank()
            for kt in range(2):
                tok = mm(b[:, 0:T], V[:, kt, h * 128:(h + 1) * 128], aT[h % 2][:, kt, :], kt == 0, kt == 1, t, free, inc=(kt == 1))
            aT_free[h % 2] = tok
            wk_free[i] = A_(o2[:, h, :], b[:, 0:T], ACT.Copy, tok)
        ts(sm("subln_g"), sm("subln_g"), 1.0 - (0.8 - 0.6), None, MUL, None)
        for p in range(4):
            rs, t, r = stat(o2[:, 2 * p:2 * p + 2, :], cs("ones128"), 2, [[0], [1]])
            for j in range(2):
                t2 = stt(o2[:, 2 * p + j, :], o2[:, 2 * p + j, :], sm("subln_g"), rs[j], MUL, MUL, t)
            rs_free[r] = t2
        t_o2 = dve.last
        tok = project(A["u_o"], o2, t_o2)

        xtok = norm_add(acc3, ng(0, 3), tok)
        ffn(0, 1, xtok)
        ple(0)
        ffn(1, 0, [dve.last] * 8)

        fence("scr")
        S4 = Scr()
        S4.at = 1536
        r_ = S4.get(32)
        phi = S4.get(32)
        wre, wim = S4.get(32), S4.get(32)
        tA, tB, tC, tE = S4.get(32), S4.get(32), S4.get(32), S4.get(32)
        Bre, Bim = S4.get(8, 128), S4.get(8, 128)
        Cre, Cim, Cx, Cy = S4.get(32, 32), S4.get(32, 32), S4.get(32, 32), S4.get(32, 32)
        t_B = [load(x, A[n], dve.last, act.last, pe.last) for x, n in ((Bre, "sBre"), (Bim, "sBim"), (Cx, "sCre"), (Cy, "sCim"))]
        th, nn, tmpa = ([S4.get(T) for _ in range(2)] for _ in range(3))
        tab = [S4.get(2, T) for _ in range(3)]
        pr, pq, ww = ([S4.get(2, T) for _ in range(2)] for _ in range(3))
        md = [S4.get(4, T) for _ in range(3)]
        t_h = norm_in(hT, xT, ng(1, 2))

        t = A_(tA, sm("log_dt"), ACT.Exp)
        tt(tB, sm("lam_re"), tA, MUL, t)
        t = tt(tC, sm("lam_im"), tA, MUL)
        t = A_(r_, tB, ACT.Exp, t)
        ts(phi, tC, 1.0 / TWO_PI, None, MUL, None)

        def frac(dst, src, tmp):
            ts(tmp, src, MAGIC, None, ADD, None)
            ts(tmp, tmp, MAGIC, None, SUB, None)
            return tt(dst, src, tmp, SUB)

        def sincos(s_out, c_out, f, tmp, *toks):
            A_(s_out, f, ACT.Sin, *toks, scale=TWO_PI * (1 - 1e-7))
            A_(tmp, f, ACT.Abs)
            return A_(c_out, tmp, ACT.Sin, scale=-TWO_PI, bias=cs("halfpi"))

        t = frac(tE, phi, wre)
        t = sincos(tC, tB, tE, wim, t)
        ta = tt(tB, r_, tB, MUL, t)
        tt(tC, r_, tC, MUL)
        ts(tB, tB, -1.0, None, ADD, None)
        lr, li = sm("lam_re"), sm("lam_im")
        tt(tA, lr, lr, MUL)
        tt(tE, li, li, MUL)
        tt(tA, tA, tE, ADD)
        recip(tA, tA)
        tt(wre, tB, lr, MUL)
        tt(tE, tC, li, MUL)
        tt(wre, wre, tE, ADD)
        tt(wre, wre, tA, MUL)
        tt(wim, tC, lr, MUL)
        tt(tE, tB, li, MUL)
        tt(wim, wim, tE, SUB)
        tt(wim, wim, tA, MUL)
        wr3 = wre.rearrange("p (a o) -> p a o", o=1).broadcast_to([128, 32, 32])
        wi3 = wim.rearrange("p (a o) -> p a o", o=1).broadcast_to([128, 32, 32])
        for tb in t_B:
            dve.wait(tb)
            pe.wait(tb)
        tt(Cre, Cx, wr3, MUL)
        tt(Cim, Cy, wi3, MUL)
        tt(Cre, Cre, Cim, SUB)
        tt(Cim, Cx, wi3, MUL)
        tt(Cx, Cy, wr3, MUL)
        tt(Cim, Cim, Cx, ADD)
        t_C = ts(Cy, Cim, -1.0, None, MUL, None)
        ts(Cx, Cre, -1.0, None, MUL, None)
        t_C = dve.last
        tab_free = [None] * 3
        th_free = [None] * 2
        ww_free = [None] * 2
        md_free = [None] * 3
        tab_tok, in_tok = {}, {}

        def tables(s):
            ph, th_, nn_ = phi[:, s:s + 1], th[s % 2], nn[s % 2]
            ts(nn_, cs("tvec"), ph, MAGIC, MUL, ADD)
            ts(nn_, nn_, MAGIC, None, SUB, None)
            t = stt(th_, cs("tvec"), ph, nn_, MUL, SUB, th_free[s % 2])
            tb = tab[s % 3]
            tab_tok[s] = sincos(tb[:, 1, :], tb[:, 0, :], th_, tmpa[s % 2], t, tab_free[s % 3])
            th_free[s % 2] = tab_tok[s]

        def drive(s):
            k, rr = s // 4, slice(32 * (s % 4), 32 * (s % 4) + 32)
            i, b, free = bank()
            for a, Bt in enumerate((Bre, Bim)):
                tok = mm(b[:, a * T:(a + 1) * T], Bt[rr, k, :], hT[rr, k, :], True, True, t_h, free, inc=(a == 1))
            in_tok[s] = (i, b, tok)

        for s in range(2):
            tables(s)
            drive(s)
        for s in range(32):
            k, j = s // 4, s % 4
            x2, x3 = s % 2, s % 3
            rr = slice(32 * j, 32 * j + 32)
            i, b, tok = in_tok[s]
            c1, s1 = (bc(tab[x3][:, a, :], 2) for a in range(2))
            v = b[:, :].rearrange("p (a t) -> p a t", a=2)
            P, Q, W, M = pr[x2], pq[x2], ww[x2], md[x3]
            tt(P, v, c1, MUL, tok, tab_tok[s])
            t = tt(Q, v, s1, MUL)
            wk_free[i] = t
            tt(P[:, 0, :], P[:, 0, :], Q[:, 1, :], ADD)
            tt(P[:, 1, :], P[:, 1, :], Q[:, 0, :], SUB)
            rb_ = r_[:, s:s + 1].broadcast_to([128, T])
            for a in range(2):
                t = dve.do(lambda e, a=a, P=P, W=W, rb_=rb_: e.tensor_tensor_scan(W[:, a, :], rb_, P[:, a, :], 0.0, MUL, ADD),
                           ww_free[x2], dve.last)
            tt(M[:, 0:2, :], W, c1, MUL, t, md_free[x3], eng=pool)
            t = tt(M[:, 2:4, :], W, s1, MUL, eng=pool)
            ww_free[x2] = tab_free[x3] = t
            if s + 2 < 32:
                tables(s + 2)
                drive(s + 2)
            dst = acc[rr, k // 2, (k % 2) * T:(k % 2 + 1) * T]
            for a, Cc in enumerate((Cre, Cy, Cy, Cx)):
                tok = mm(dst, Cc[:, s, :], M[:, a, :], k % 2 == 0 and a == 0, a == 3, t, t_C, acc_free[0],
                         inc=(a == 3), skip=True)
            md_free[x3] = tok
        for k in range(8):
            t = stt(sq[:, k, :], hT[:, k, :], sm("ssm_d", k, k + 1), acc3[:, k, :], MUL, ADD, tok)
        acc_free[0] = t
        t_y = A_(hT[:, :, :], sq[:, :, :], ACT.Gelu_apprx_tanh, t)
        S5 = Scr()
        S5.at = 1536 + 512
        fence()
        zz = S5.get(8, T)
        zs = S5.get(2, T)
        for u in range(4):
            ub, wb, twb = chunk(A["u_glu"][2 * u])
            un, wg, tw = chunk(A["u_glu"][2 * u + 1])

            def ev_gate(i0, n, b, tok):
                for j in range(2):
                    c = 2 * u + j
                    t = A_(zs[:, j, :], b[:, j * T:(j + 1) * T], ACT.Sigmoid, tok, dve.last, bias=sm("b_glu", 8 + c, 9 + c))
                return t

            def ev_val(i0, n, b, tok):
                for j in range(2):
                    c = 2 * u + j
                    t = stt(zz[:, c, :], b[:, j * T:(j + 1) * T], sm("b_glu", c, c + 1), zs[:, j, :], ADD, MUL, tok, act.last)
                return t

            lin_fm(lambda k, c: wb[:, k, c * 128:(c + 1) * 128], 8, lambda k: hT[:, k, :], 2, ev_gate, twb, t_y)
            release(ub, pe.last)
            lin_fm(lambda k, c: wg[:, k, c * 128:(c + 1) * 128], 8, lambda k: hT[:, k, :], 2, ev_val, tw, t_y)
            release(un, pe.last)
        rs, t, r = stat(zz, cs("onesD"), 8, [list(range(8))], dve.last)
        g = ng(1, 3)

        for k in range(8):
            t2 = stt(hT[:, k, :], zz[:, k, :], g[:, k:k + 1], rs[0], MUL, MUL, t, pe.last)
        rs_free[r] = t2
        tt(xT[:, :, :], xT[:, :, :], hT[:, :, :], ADD, t2)
        ffn(1, 1, [dve.last] * 8)
        ple(1)
        finish()
        return emit()


def _ktile(w, cols=None):
    K, N = w.shape
    return np.ascontiguousarray(w.reshape(K // 128, 128, N).transpose(1, 0, 2).reshape(128, -1))


def _glu_units(wg, wu, wd, side=False):
    n, _, F = wg.shape
    f = F // 128
    out = np.empty((n, f, 128, UNIT), wg.dtype)
    for a, w in enumerate((wg, wu)):
        out[..., a * 1024:(a + 1) * 1024] = w.reshape(n, 8, 128, f, 128).transpose(0, 3, 2, 1, 4).reshape(n, f, 128, 1024)
    if side:
        out[..., :2048] = out[..., :2048].reshape(n, f, 128, 2, 8, 128).transpose(0, 1, 2, 4, 3, 5).reshape(n, f, 128, 2048)
    out[..., 2048:] = wd.reshape(n, f, 128, 1024)
    return out.reshape(n * f, 128, UNIT)


def _chunks(w):
    return np.stack([_ktile(w[:, c:c + 256]) for c in range(0, w.shape[1], 256)])


def _feat(v):
    return v.reshape(-1, 8, 128).transpose(2, 0, 1).reshape(128, -1)


def _constants():
    c = np.zeros((128, NCC), np.float32)

    def put(name, v):
        a, b = CCOL[name]
        c[:, a:b] = v

    p = np.arange(128)
    put("ident", np.eye(128))
    put("anti", np.eye(128)[::-1])
    put("onesD", 1.0 / 1024)
    put("onesB", (p[:, None] // 64 == p[None, :] // 64) / 64.0)
    put("ones128", 1.0 / 128)
    put("mask", (p[:, None] // 64 == p[None, :] // 64) & (p[:, None] <= p[None, :]))
    put("tiew", 8.0 - np.arange(8))
    put("before", p[:, None] < p[None, :])
    put("ones", 1.0)
    put("eps", 1e-6)
    put("halfpi", math.pi / 2)
    put("scanm", np.arange(256) % 64 != 0)
    put("tvec", np.arange(256))
    dist = 255 - np.arange(512)
    n = np.maximum(dist, 0)
    nf = np.maximum(n, 1).astype(np.float32)
    large = 16 + (np.log(nf / np.float32(16)) / np.float32(math.log(128 / 16)) * np.float32(16)).astype(np.int32)
    bucket = np.where(n < 16, n, np.minimum(large, 31))
    oh = np.zeros((128, 512), np.float32)
    oh[bucket, np.arange(512)] = 1.0
    oh[:, 511] = 0
    put("bucket", oh)
    put("cut", np.where(dist >= 0, 0.0, NEG)[None, :])
    slopes = (2.0 ** (-8.0 * np.arange(1, 5) / 4)).astype(np.float32)
    q = np.arange(256).reshape(2, 128).T
    d = (q[:, None, :, None] - np.arange(256)[None, None, None, :]).astype(np.float32)
    mb = np.where(d >= 0, -(slopes[None, :, None, None] * d), np.float32(NEG))
    return c, np.ascontiguousarray(mb.astype(np.float32).reshape(128, 4 * 512))


def _layout(i):
    f = {k: np.asarray(v) for k, v in i.items()}
    a = {}
    a["xT"] = np.ascontiguousarray(f["x"][0].T)
    a["memT"] = np.ascontiguousarray(f["mem"][0].T)
    w = f["w_in"][0]
    c = np.concatenate
    a["u_q"] = _ktile(c([w[:, 0:256], w[:, 1536:1552]], 1))
    a["u_in"] = _chunks(c([w[:, 256:1024], w[:, 2064:2320], w[:, 1024:1536], w[:, 1552:2064], w[:, 2320:2576]], 1))
    a["u_mem"] = _chunks(f["w_mem_kv"][0])
    a["u_out"] = _chunks(f["w_out"][0])
    a["u_moe"] = _glu_units(f["w_gate"][0], f["w_up"][0], f["w_down"][0], True)
    fi = f["ffn_w_in_2"].reshape(4, 1024, 5632)
    a["u_ffn"] = _glu_units(fi[:, :, :2816], fi[:, :, 2816:], f["ffn_w_out_2"].reshape(4, 2816, 1024))
    a["u_qkv"] = _chunks(f["attn_w_qkv_2"][0])
    a["u_o"] = _chunks(f["attn_w_o_2"][0])
    wg = _chunks(f["ssm_w_glu_2"][0])
    a["u_glu"] = np.stack([wg[n] for u in range(4) for n in (4 + u, u)])
    a["u_ple"] = np.stack([c([_ktile(f["ple_w_gate_2"][i][:, h:h + 256]),
                              _ktile(f["ple_w_proj_2"][i][:, h:h + 256])], 1)
                           for i in range(2) for h in range(0, 1024, 256)])
    a["pT"] = np.ascontiguousarray(f["p_2"][:, 0].transpose(0, 2, 1))
    s = np.zeros((128, NSC), np.float32)

    def put(name, v):
        x, y = SCOL[name]
        s[0:v.shape[0], x:y] = v

    put("attn_g", _feat(f["attn_norm_g"]))
    put("mem_g", _feat(f["mem_norm_g"]))
    put("ffn_g", _feat(f["ffn_norm_g"]))
    put("b_gk", f["b_gla_gk"].reshape(2, 128).T)
    put("gla_g", f["gla_out_norm_g"].T)
    for n, k in (("mbq_g", "moba_q_norm_g"), ("mbk_g", "moba_k_norm_g"), ("mq_g", "mem_q_norm_g"), ("mk_g", "mem_k_norm_g")):
        put(n, c([f[k].T, f[k].T], 0))
    put("norm_g", _feat(f["norm_g_2"]))
    put("subln_g", f["attn_subln_g_2"].T)

    def states(v):
        return v.reshape(32, 128).T

    put("lam_re", states(f["ssm_lam_re_2"][0]))
    put("lam_im", states(f["ssm_lam_im_2"][0]))
    put("log_dt", states(np.repeat(f["ssm_log_dt_2"][0][:, None], 64, 1)))
    put("ssm_d", _feat(f["ssm_d_2"]))
    put("b_glu", f["ssm_b_glu_2"].reshape(16, 128).T)
    put("lamv", np.broadcast_to(f["attn_lam_2"].reshape(1, 256), (128, 256)))
    put("rbias", np.broadcast_to(c([f["b_router_group"], f["b_router_expert"].reshape(1, 32)], 1), (128, 36)))
    wr = c([f["w_router_group"][0], f["w_router_expert"][0].transpose(1, 0, 2).reshape(1024, 32)], 1)
    put("w_r", _ktile(wr))
    put("w_gk", f["w_gla_gk"][0])
    put("relb", f["rel_bias_2"])
    a["small"] = s
    for n, k in (("sBre", "ssm_b_re_2"), ("sBim", "ssm_b_im_2")):
        v = np.zeros((8, 4, 2, 16, 2, 64), np.float32)
        src = f[k][0].reshape(8, 4, 2, 64, 16).transpose(0, 1, 2, 4, 3)
        for g in range(2):
            v[:, :, g, :, g, :] = src[:, :, g]
        a[n] = np.ascontiguousarray(v.reshape(8, 128, 128).transpose(1, 0, 2).reshape(128, 1024))
    for n, k in (("sCre", "ssm_c_re_2"), ("sCim", "ssm_c_im_2")):
        v = np.zeros((32, 2, 64, 2, 16), np.float32)
        src = f[k][0].reshape(32, 2, 16, 64).transpose(0, 1, 3, 2)
        for g in range(2):
            v[:, g, :, g, :] = src[:, g]
        a[n] = np.ascontiguousarray(v.reshape(32, 128, 32).transpose(1, 0, 2).reshape(128, 1024))
    a["cst"], a["mbias"] = _constants()
    return a


def kernel(**inputs):
    import numpy as _np
    import concourse.bacc as _bacc
    from concourse import mybir as _mybir
    from concourse.bass_utils import run_bass_kernel_spmd as _run

    nc = _bacc.Bacc("TRN2", target_bir_lowering=False, num_devices=1)
    lay = _layout(inputs)
    arrays, A = {}, {}
    for name, a in lay.items():
        arrays[f"in_{name}"] = a
        A[name] = nc.dram_tensor(f"in_{name}", a.shape, _mybir.dt.from_np(a.dtype), kind="ExternalInput").ap()
    for name in ("sBre", "sBim"):
        A[name] = A[name].rearrange("p (a b) -> p a b", a=8)
    for name in ("sCre", "sCim"):
        A[name] = A[name].rearrange("p (a b) -> p a b", a=32)
    A["mbias"] = A["mbias"].rearrange("p (a b) -> p a b", a=4)
    A["rscratch"] = nc.dram_tensor("rscratch", (16, 512), F32, kind="Internal").ap()
    out = nc.dram_tensor("out_0", (D, T), F32, kind="ExternalOutput").ap()
    program(nc, A, out)
    r = _run(nc, [arrays], core_ids=[0])
    got = r.results[0]["out_0"]
    return _np.ascontiguousarray(got.T).reshape(1, T, D)
```
